# Optimizing a Trainium2 kernel written in Bass

```python
import jax, jax.numpy as jnp
from jax import lax
import numpy as np

'''One inference step (DEPTH layers) of a conditioned hybrid decoder with parallel head groups.

Each layer: adaLN-modulated RMSNorm -> one combined input projection whose columns are split
into [u | v] for a chunked causal spatial-gating mixer (4 heads x 128) and [p] for a
multi-scale causal pooling mixer (4 channel groups x 128, windows 2/4/8/16). The two branch
outputs are RMS-normalised, concatenated and sent through one output projection, then added
with an adaLN gate. Then adaLN-modulated RMSNorm -> dense SwiGLU (even layers) or top-2-of-8
expert SwiGLU (odd layers), gated residual add. One final RMSNorm.

Inputs:
  x_prompt   (BATCH, SEQ, D_MODEL)          positions 0..SEQ-1
  x_sample   (DEC_BATCH, DEC_SEQ, D_MODEL)  positions PAST_LEN..PAST_LEN+DEC_SEQ-1
  state_pool (DEPTH, DEC_BATCH, POOL_BUF, POOL_WIDTH)  last 15 pooling-branch input rows
  c_prompt   (BATCH, D_MODEL), c_sample (DEC_BATCH, D_MODEL)  conditioning vectors
  + weights (shared by both groups)
Returns (y_prompt, y_sample, pool_state_prompt, pool_state_sample, chunk_v_prompt, chunk_v_sample):
  y_prompt          (BATCH, SEQ, D_MODEL)
  y_sample          (DEC_BATCH, DEC_SEQ, D_MODEL)
  pool_state_prompt (DEPTH, BATCH, POOL_BUF, POOL_WIDTH)      last 15 pooling inputs of each prompt
  pool_state_sample (DEPTH, DEC_BATCH, POOL_BUF, POOL_WIDTH)  updated pooling buffer of each sample
  chunk_v_prompt    (DEPTH, BATCH, CHUNK, SGU_WIDTH)          normalised v rows of the final prompt chunk
  chunk_v_sample    (DEPTH, DEC_BATCH, DEC_SEQ, SGU_WIDTH)    normalised v rows of the new open chunk
'''

D_MODEL = 1024
BATCH = 1
SEQ = 256
DEPTH = 2
DEC_BATCH = 8
DEC_SEQ = 8
PAST_LEN = 2048
PAGE_SIZE = 128

MIX_WIDTH = D_MODEL
SGU_HEADS = 4
SGU_WIDTH = MIX_WIDTH // 2
SGU_HEAD_DIM = SGU_WIDTH // SGU_HEADS
CHUNK = 128
POOL_WINDOWS = (2, 4, 8, 16)
POOL_GROUPS = len(POOL_WINDOWS)
POOL_WIDTH = MIX_WIDTH - SGU_WIDTH
POOL_GROUP_DIM = POOL_WIDTH // POOL_GROUPS
POOL_BUF = max(POOL_WINDOWS) - 1
IN_WIDTH = 2 * SGU_WIDTH + POOL_WIDTH
D_FF = 7 * D_MODEL // 2
N_EXPERTS = 8
TOP_K = 2
N_DENSE = (DEPTH + 1) // 2
N_MOE = DEPTH // 2
EPS = 1e-6

kernel_name = 'hybrid_sgu_pool_adaln_decoder_step'

def rmsnorm(x, g):
    xf = x.astype(jnp.float32)
    xf = xf * lax.rsqrt(jnp.mean(xf * xf, axis=-1, keepdims=True) + EPS)
    return xf.astype(x.dtype) * g

def head_layernorm(v, g, b):
    B, L, _ = v.shape
    vf = v.astype(jnp.float32).reshape(B, L, SGU_HEADS, SGU_HEAD_DIM)
    mu = jnp.mean(vf, axis=-1, keepdims=True)
    var = jnp.mean(jnp.square(vf - mu), axis=-1, keepdims=True)
    vn = ((vf - mu) * lax.rsqrt(var + EPS)).reshape(B, L, SGU_WIDTH)
    return vn.astype(v.dtype) * g + b

def adaln_params(c, w, b):
    mod = jax.nn.silu(c) @ w + b
    return jnp.split(mod[:, None, :], 6, axis=-1)

def modulate(x, g, shift, scale):
    return rmsnorm(x, g) * (1 + scale) + shift

def chunk_sgu(u, v_raw, g, b, sgu_w, sgu_b, chunk):
    B, L, _ = v_raw.shape
    v = head_layernorm(v_raw, g, b)
    vc = v.reshape(B, L // chunk, chunk, SGU_HEADS, SGU_HEAD_DIM)
    mask = jnp.tril(jnp.ones((chunk, chunk), dtype=bool))
    w = jnp.where(mask[None], sgu_w[:, :chunk, :chunk], 0).astype(v.dtype)
    bias = sgu_b[:, :chunk].T[None, None, :, :, None]
    mixed = jnp.einsum('hts,bnshd->bnthd', w, vc) + bias
    y = u * mixed.reshape(B, L, SGU_WIDTH)
    return y, v

def pool_mix(buf, p, pos, pool_w, pool_scale):
    B, L, _ = p.shape
    xpad = jnp.concatenate([buf.astype(p.dtype), p], axis=1)
    cs = jnp.cumsum(xpad.astype(jnp.float32), axis=1)
    cs = jnp.concatenate([jnp.zeros((B, 1, POOL_WIDTH), jnp.float32), cs], axis=1)
    pf = p.astype(jnp.float32)
    outs = []
    for gi, win in enumerate(POOL_WINDOWS):
        lo, hi = gi * POOL_GROUP_DIM, (gi + 1) * POOL_GROUP_DIM
        wsum = cs[:, POOL_BUF + 1:, lo:hi] - cs[:, POOL_BUF + 1 - win:POOL_BUF + 1 - win + L, lo:hi]
        cnt = jnp.minimum(win, pos + 1).astype(jnp.float32)[None, :, None]
        outs.append(wsum / cnt - pf[:, :, lo:hi])
    d = jnp.concatenate(outs, axis=-1).astype(p.dtype).reshape(B, L, POOL_GROUPS, POOL_GROUP_DIM)
    y = jnp.einsum('blgc,gcd->blgd', d, pool_w).reshape(B, L, POOL_WIDTH) * pool_scale
    return y, xpad[:, -POOL_BUF:]

def swiglu(h, w1, w3, w2):
    return (jax.nn.silu(h @ w1) * (h @ w3)) @ w2

def moe_swiglu(h, router_w, w1, w3, w2):
    B, L, D = h.shape
    t = h.reshape(B * L, D)
    logits = (t @ router_w).astype(jnp.float32)
    top_v, top_i = lax.top_k(logits, TOP_K)
    gates = jax.nn.softmax(top_v, axis=-1)
    out = jnp.zeros((B * L, D), jnp.float32)
    for e in range(N_EXPERTS):
        w_e = jnp.sum(jnp.where(top_i == e, gates, 0.0), axis=-1)
        out = out + w_e[:, None] * swiglu(t, w1[e], w3[e], w2[e]).astype(jnp.float32)
    return out.astype(h.dtype).reshape(B, L, D)

def setup_inputs(seed: int = 0) -> dict:
    key = jax.random.key(seed)
    ks = jax.random.split(key, 32)
    f32 = jnp.float32
    nrm = lambda k, shape, s: jax.random.normal(k, shape, f32) * s
    gain = lambda k, shape: 1.0 + nrm(k, shape, 0.02)
    return {
        'x_prompt': nrm(ks[0], (BATCH, SEQ, D_MODEL), 1.0),
        'x_sample': nrm(ks[1], (DEC_BATCH, DEC_SEQ, D_MODEL), 1.0),
        'state_pool': nrm(ks[2], (DEPTH, DEC_BATCH, POOL_BUF, POOL_WIDTH), 1.0),
        'c_prompt': nrm(ks[3], (BATCH, D_MODEL), 1.0),
        'c_sample': nrm(ks[4], (DEC_BATCH, D_MODEL), 1.0),
        'norm1_g': gain(ks[5], (DEPTH, D_MODEL)),
        'norm2_g': gain(ks[6], (DEPTH, D_MODEL)),
        'ada_w': nrm(ks[7], (DEPTH, D_MODEL, 6 * D_MODEL), 0.5 * D_MODEL ** -0.5),
        'ada_b': nrm(ks[8], (DEPTH, 6 * D_MODEL), 0.02),
        'w_in': nrm(ks[9], (DEPTH, D_MODEL, IN_WIDTH), D_MODEL ** -0.5),
        'v_norm_g': gain(ks[10], (DEPTH, SGU_WIDTH)),
        'v_norm_b': nrm(ks[11], (DEPTH, SGU_WIDTH), 0.02),
        'sgu_w': nrm(ks[12], (DEPTH, SGU_HEADS, CHUNK, CHUNK), CHUNK ** -0.5),
        'sgu_b': 1.0 + nrm(ks[13], (DEPTH, SGU_HEADS, CHUNK), 0.1),
        'pool_w': nrm(ks[14], (DEPTH, POOL_GROUPS, POOL_GROUP_DIM, POOL_GROUP_DIM), POOL_GROUP_DIM ** -0.5),
        'pool_scale': 1.0 + nrm(ks[15], (DEPTH, POOL_WIDTH), 0.1),
        'branch_a_g': gain(ks[16], (DEPTH, SGU_WIDTH)),
        'branch_b_g': gain(ks[17], (DEPTH, POOL_WIDTH)),
        'w_out': nrm(ks[18], (DEPTH, MIX_WIDTH, D_MODEL), MIX_WIDTH ** -0.5),
        'ffn_w1': nrm(ks[19], (N_DENSE, D_MODEL, D_FF), D_MODEL ** -0.5),
        'ffn_w3': nrm(ks[20], (N_DENSE, D_MODEL, D_FF), D_MODEL ** -0.5),
        'ffn_w2': nrm(ks[21], (N_DENSE, D_FF, D_MODEL), D_FF ** -0.5),
        'router_w': nrm(ks[22], (N_MOE, D_MODEL, N_EXPERTS), D_MODEL ** -0.5),
        'moe_w1': nrm(ks[23], (N_MOE, N_EXPERTS, D_MODEL, D_FF), D_MODEL ** -0.5),
        'moe_w3': nrm(ks[24], (N_MOE, N_EXPERTS, D_MODEL, D_FF), D_MODEL ** -0.5),
        'moe_w2': nrm(ks[25], (N_MOE, N_EXPERTS, D_FF, D_MODEL), D_FF ** -0.5),
        'final_g': gain(ks[26], (D_MODEL,)),
    }

def reference(x_prompt, x_sample, state_pool, c_prompt, c_sample, norm1_g, norm2_g, ada_w, ada_b,
              w_in, v_norm_g, v_norm_b, sgu_w, sgu_b, pool_w, pool_scale, branch_a_g, branch_b_g,
              w_out, ffn_w1, ffn_w3, ffn_w2, router_w, moe_w1, moe_w3, moe_w2, final_g):
    pos_p = jnp.arange(x_prompt.shape[1], dtype=jnp.int32)
    pos_s = PAST_LEN + jnp.arange(x_sample.shape[1], dtype=jnp.int32)
    buf_p0 = jnp.zeros((x_prompt.shape[0], POOL_BUF, POOL_WIDTH), x_prompt.dtype)

    def run_layer(l, x, c, buf, pos, chunk):
        sh1, sc1, gt1, sh2, sc2, gt2 = adaln_params(c, ada_w[l], ada_b[l])
        h = modulate(x, norm1_g[l], sh1, sc1)
        z = h @ w_in[l]
        u = jax.nn.gelu(z[..., :SGU_WIDTH])
        v_raw = jax.nn.gelu(z[..., SGU_WIDTH:2 * SGU_WIDTH])
        p = z[..., 2 * SGU_WIDTH:]
        ya, v = chunk_sgu(u, v_raw, v_norm_g[l], v_norm_b[l], sgu_w[l], sgu_b[l], chunk)
        yb, new_buf = pool_mix(buf, p, pos, pool_w[l], pool_scale[l])
        mix = jnp.concatenate([rmsnorm(ya, branch_a_g[l]), rmsnorm(yb, branch_b_g[l])], axis=-1) @ w_out[l]
        x = x + gt1 * mix
        h = modulate(x, norm2_g[l], sh2, sc2)
        if l % 2 == 0:
            f = swiglu(h, ffn_w1[l // 2], ffn_w3[l // 2], ffn_w2[l // 2])
        else:
            f = moe_swiglu(h, router_w[l // 2], moe_w1[l // 2], moe_w3[l // 2], moe_w2[l // 2])
        x = x + gt2 * f
        return x, new_buf, v

    xp, xs = x_prompt, x_sample
    bufs_p, bufs_s, vs_p, vs_s = [], [], [], []
    for l in range(DEPTH):
        xp, bp, vp = run_layer(l, xp, c_prompt, buf_p0, pos_p, CHUNK)
        xs, bs, vsm = run_layer(l, xs, c_sample, state_pool[l], pos_s, x_sample.shape[1])
        bufs_p.append(bp)
        bufs_s.append(bs)
        vs_p.append(vp[:, -CHUNK:])
        vs_s.append(vsm)
    y_prompt = rmsnorm(xp, final_g)
    y_sample = rmsnorm(xs, final_g)
    pool_state_prompt = jnp.stack(bufs_p, axis=0)
    pool_state_sample = jnp.stack(bufs_s, axis=0)
    chunk_v_prompt = jnp.stack(vs_p, axis=0)
    chunk_v_sample = jnp.stack(vs_s, axis=0)
    return (y_prompt, y_sample, pool_state_prompt, pool_state_sample, chunk_v_prompt, chunk_v_sample)


_drawn_inputs = setup_inputs


def setup_inputs(seed=0):
    import zlib

    import numpy as np

    out = dict(_drawn_inputs(seed))
    spreads = {}
    factors = {'norm2_g': 3.449,
     'v_norm_g': 2.907,
     'v_norm_b': 2.82,
     'branch_a_g': 6.145,
     'branch_b_g': 6.316,
     'final_g': 2.777}
    for name, (base, spread) in spreads.items():
        noise = np.random.default_rng([zlib.crc32(name.encode()), seed]).standard_normal(out[name].shape)
        drawn = base * np.exp(spread * noise) if base else spread * noise
        out[name] = __import__('jax').numpy.asarray(drawn.astype(out[name].dtype))
    for name, factor in factors.items():
        out[name] = (out[name] * factor).astype(out[name].dtype)
    return out
```

```python
from contextlib import ExitStack

import numpy as np

import concourse.bass as bass
import concourse.mybir as mybir

F32 = mybir.dt.float32
F32R = mybir.dt.float32r
I32 = mybir.dt.int32
U32 = mybir.dt.uint32
ALU = mybir.AluOpType
ACT = mybir.ActivationFunctionType
AX = mybir.AxisListType

P = 128
D = 1024
KD = D // P
DEPTH = 2
NP_TOK = 256
NSEQ = 8
TS = 8
NS_TOK = NSEQ * TS
T = NP_TOK + NS_TOK
VBLK = (0, P, T - P)
BLK = [P, P, NS_TOK]
NBLK = len(BLK)
ROWS = 1 + NSEQ
NMOD = 6 * KD
H = 4
HALF = 512
BUF = 15
WIN = (2, 4, 8, 16)
BIAS_ROW = 96
PADP = 16
DFF = 3584
B = 512
KB = B // P
NSTEP = DFF // B
E = 8
EPS = 1e-6
NV = 84
R_N1, R_N2, R_ADAB, R_PS, R_AG, R_BG, R_FG = 0, 8, 16, 64, 68, 72, 76

RAW = 6
SPL = 3
EXTRA_MAX = 4

N_ADA, N_IN, N_OUT, N_FFN = 24, 6, 4, 6 * NSTEP
U_ADA = (0, N_ADA + N_IN)
U_IN = (N_ADA, 2 * N_ADA + N_IN + N_OUT + N_FFN)
U_OUT = (2 * N_ADA + N_IN, U_IN[1] + N_IN)
U_FFN = U_OUT[0] + N_OUT
U_MOE = U_OUT[1] + N_OUT
S_IN = (0, N_IN + N_OUT + N_FFN)
S_OUT = (N_IN, S_IN[1] + N_IN)
S_FFN = N_IN + N_OUT
S_MOE = S_OUT[1] + N_OUT


def kind(u):
    if u < N_ADA:
        return True, u
    if u < U_ADA[1]:
        return False, u - N_ADA
    if u < U_ADA[1] + N_ADA:
        return True, u - U_ADA[1] + N_ADA
    return False, u - 2 * N_ADA


def unit_of_split(s):
    return s + (N_ADA if s < N_IN else 2 * N_ADA)


def build_program(nc):
    shapes = {
        'x_prompt': (1, NP_TOK, D), 'x_sample': (NSEQ, TS, D), 'state_pool': (DEPTH, NSEQ, BUF, HALF),
        'c_prompt': (1, D), 'c_sample': (NSEQ, D), 'norm1_g': (DEPTH, D), 'norm2_g': (DEPTH, D),
        'ada_w': (DEPTH, D, 6 * D), 'ada_b': (DEPTH, 6 * D), 'w_in': (DEPTH, D, 3 * HALF),
        'v_norm_g': (DEPTH, HALF), 'v_norm_b': (DEPTH, HALF), 'sgu_w': (DEPTH, H, P, P), 'sgu_b': (DEPTH, H, P),
        'pool_w': (DEPTH, H, P, P), 'pool_scale': (DEPTH, HALF), 'branch_a_g': (DEPTH, HALF),
        'branch_b_g': (DEPTH, HALF), 'w_out': (DEPTH, D, D), 'ffn_w1': (1, D, DFF), 'ffn_w3': (1, D, DFF),
        'ffn_w2': (1, DFF, D), 'router_w': (1, D, E), 'moe_w1': (1, E, D, DFF), 'moe_w3': (1, E, D, DFF),
        'moe_w2': (1, E, DFF, D), 'final_g': (D,),
    }
    out_shapes = [(1, NP_TOK, D), (NSEQ, TS, D), (DEPTH, 1, BUF, HALF), (DEPTH, NSEQ, BUF, HALF),
                  (DEPTH, 1, P, HALF), (DEPTH, NSEQ, TS, HALF)]
    d = {n: nc.dram_tensor(f"in_{n}", s, F32, kind="ExternalInput").ap() for n, s in shapes.items()}
    o = [nc.dram_tensor(f"out_{i}", s, F32, kind="ExternalOutput").ap() for i, s in enumerate(out_shapes)]
    with ExitStack() as ctx:
        write_program(nc, ctx, d, o)


def write_program(nc, ctx, d, o):
    def sb(name, shape, dt=F32):
        return ctx.enter_context(nc.sbuf_tensor(name, shape, dt))

    def sem(name):
        return ctx.enter_context(nc.semaphore(name))

    raw = sb("raw", [P, RAW, KB, B])
    w_hi = sb("w_hi", [P, SPL, KB, B], F32R)
    w_lo = sb("w_lo", [P, SPL, KB, B], F32R)
    x = sb("x", [P, KD, T])
    hf = sb("hf", [P, KD, T])
    sq = hf
    rstd = sb("rstd", [P, T])
    stdt = rstd
    mod = sb("mod", [P, DEPTH, NMOD, ROWS])
    gain = sb("gain", [P, DEPTH, 2, KD, ROWS])
    modrow = sb("modrow", [ROWS, B])
    cT = sb("cT", [P, KD, ROWS])
    vec = sb("vec", [P, DEPTH, NV])
    ident = sb("ident", [P, P])
    ones = sb("ones", [P, P])
    below = sb("below", [P, P])
    iota = sb("iota", [P, P])
    eps = sb("eps", [P, 1])
    vng = sb("vng", [P, HALF])
    vnb = sb("vnb", [P, HALF])
    pw = sb("pw", [P, H, P])
    gw = sb("gw", [P, DEPTH, H, P])
    gs = sb("gs", [P, DEPTH, H, NS_TOK])
    pp = sb("pp", [P, H, PADP + NP_TOK])
    sp_ = sb("sp_", [P, DEPTH, H, NSEQ, BUF + TS])
    rcnt = sb("rcnt", [P, H, PADP])
    first = sb("first", [P, H, PADP])
    pst = sb("pst", [P, HALF])
    g_bias = pst[BIAS_ROW:BIAS_ROW + 1].rearrange("p (h t) -> p h t", t=P)
    v_stat = sb("v_stat", [P, NBLK * H, 6])
    v_mv = sb("v_mv", [P, NBLK * H, 2])
    v_std = sb("v_std", [P, NBLK * H])
    v_rstd = sb("v_rstd", [P, NBLK * H])
    smp = sb("smp", [P, 2, NS_TOK])
    rw = sb("rw", [P, KD, E])
    logit = sb("logit", [P, NBLK, E])
    top = sb("top", [P, NBLK, 8])
    topi = sb("topi", [P, NBLK, 8], U32)
    topf = sb("topf", [P, NBLK, 8])
    oh = sb("oh", [P, 2, NBLK, E])
    chosen = sb("chosen", [P, NBLK, E])
    rank = sb("rank", [P, NBLK, E])
    over1 = sb("over1", [P, NBLK, E])
    posn = sb("posn", [P, NBLK, E])
    tmpe = sb("tmpe", [P, NBLK, E])
    pos = sb("pos", [P, 2, NBLK])
    gate = sb("gate", [P, 2, NBLK])
    dtop = sb("dtop", [P, NBLK])
    etop = sb("etop", [P, NBLK])
    dsum = sb("dsum", [P, NBLK])
    cnt = sb("cnt", [P, E])
    ext = sb("ext", [P, E])
    ext2 = sb("ext2", [P, E])
    ebase = sb("ebase", [P, E])
    eoff = sb("eoff", [P, E])
    tab = sb("tab", [P, EXTRA_MAX + 1])
    inj = sb("inj", [P, E])
    inj2 = sb("inj2", [P, E])
    table = sb("table", [P, EXTRA_MAX + 1], I32)

    def views(name, dt, *phases):
        size = max(sum(int(np.prod(sh)) for sh in ph) for ph in phases)
        area = sb(name, [P, size], dt)
        out = []
        for ph in phases:
            at, got = 0, []
            for sh in ph:
                n = int(np.prod(sh))
                v = area[:, at:at + n]
                if len(sh) == 2:
                    v = v.rearrange("p (a b) -> p a b", b=sh[1])
                elif len(sh) == 3:
                    v = v.rearrange("p (a b c) -> p a b c", b=sh[1], c=sh[2])
                got.append(v)
                at += n
            out.append(got)
        return out

    (h_hi, h_lo, g_hi, g_lo), (ht_hi, ht_lo, xs_hi, xs_lo, gt_hi, gt_lo, sel) = views(
        "split", F32R,
        [(KD, T), (KD, T), (KB, T), (KB, T)],
        [(NBLK, D), (NBLK, D), (KD, P), (KD, P), (KB, P), (KB, P), (NBLK, P)])
    ((_, xtok, gw_raw, gs_raw, buf_raw), (uT, v_gelu, v_norm, wa, wb, wsa, wsb), (facc, _, silu_t),
     (_, _, e_silu, e_g, e_y, gat, gat1, gatT)) = views(
        "plain", F32,
        [(H, T), (NBLK, D), (DEPTH * H, P), (DEPTH * H, P), (DEPTH, HALF)],
        [(H, T), (NBLK, HALF), (NBLK, HALF), (H, PADP + NP_TOK), (H, PADP + NP_TOK),
         (H, NSEQ, BUF + TS), (H, NSEQ, BUF + TS)],
        [(KD, T), (H * T + NBLK * D - KD * T,), (KB, T)],
        [(KD, T), (H * T + NBLK * D - KD * T,), (B,), (B,), (D,), (NBLK, P), (NBLK, P), (T,)])
    g_f = silu_t
    yb = v_gelu.rearrange("p a b -> p (a b)")[:, 0:H * T].rearrange("p (a b) -> p a b", b=T)
    hrow = hf[:].rearrange("p a b -> p (a b)")
    crow, cs_row = hrow[0:ROWS, 0:D], hrow[0:ROWS, D:2 * D]
    vrow = hrow[0:NV, 2 * D:2 * D + DEPTH * P].rearrange("p (a b) -> p a b", b=P)
    sps = hrow[:, 0:H * NS_TOK].rearrange("p (h t) -> p h t", t=NS_TOK)
    iota_i = rstd[:, 0:P].bitcast(I32)

    ps = ctx.enter_context(nc.psum_tensor("ps", [P, 8, 512], F32))

    raw_in = [sem(f"raw_in{i}") for i in range(RAW)]
    hi_ready = sem("hi_ready")
    lo_ready = sem("lo_ready")
    split_used = sem("split_used")
    plain_used = sem("plain_used")
    c_in = sem("c_in")
    vec_in = sem("vec_in")
    x_in = sem("x_in")
    aux_in = sem("aux_in")
    gw_in = sem("gw_in")
    rw_in = sem("rw_in")
    y_stored = sem("y_stored")
    zeroed = sem("zeroed")
    const = sem("const")
    pool_step = sem("pool_step")
    dve = sem("dve")
    act_c = sem("act_c")
    prep_tr = sem("prep_tr")
    prep_cp = sem("prep_cp")
    masked = sem("masked")
    row_out = sem("row_out")
    row_tr = sem("row_tr")
    mod_add = sem("mod_add")
    mod_ready = sem("mod_ready")
    x_cp = sem("x_cp")
    x_new = sem("x_new")
    sq_ready = sem("sq_ready")
    ssum = sem("ssum")
    std_ready = sem("std_ready")
    scaled = sem("scaled")
    affine = sem("affine")
    hhi = sem("hhi")
    h_ready = sem("h_ready")
    u_out = sem("u_out")
    v_out = sem("v_out")
    p_out = sem("p_out")
    v_var = sem("v_var")
    v_sd = sem("v_sd")
    v_done = sem("v_done")
    win_s = sem("win_s")
    d_done = sem("d_done")
    gate_mm = sem("gate_mm")
    ya_done = sem("ya_done")
    pool_mm = sem("pool_mm")
    yb_done = sem("yb_done")
    st_tr = sem("st_tr")
    st_cp = sem("st_cp")
    stored = sem("stored")
    v_stored = sem("v_stored")
    f_silu = sem("f_silu")
    f_mul = sem("f_mul")
    f_hi = sem("f_hi")
    f_lo = sem("f_lo")
    f_add = sem("f_add")
    log_mm = sem("log_mm")
    tok_tr = sem("tok_tr")
    tok_hi = sem("tok_hi")
    tok_lo = sem("tok_lo")
    top_done = sem("top_done")
    exp_done = sem("exp_done")
    chosen_r = sem("chosen_r")
    rank_mm = sem("rank_mm")
    routed = sem("routed")
    sel_ready = sem("sel_ready")
    gat_step = sem("gat_step")
    gath = sem("gath")
    xhi = sem("xhi")
    xlo = sem("xlo")
    e_si = sem("e_si")
    e_mu = sem("e_mu")
    e_tr = sem("e_tr")
    e_hi = sem("e_hi")
    e_lo = sem("e_lo")
    gat_tr = sem("gat_tr")
    gat_cp = sem("gat_cp")
    y_cp = sem("y_cp")
    scat = sem("scat")
    scat_add = sem("scat_add")
    fin_t = sem("fin_t")
    mixed = sem("mixed")
    mixed_hi = sem("mixed_hi")
    layer_in = sem("layer_in")
    own = sem("own")
    own_end = sem("own_end")
    fin_tr = sem("fin_tr")
    fin_cp = sem("fin_cp")

    N_C, N_VEC, N_X, N_AUX = 2, 8, 3, 0

    block = ctx.enter_context(nc.Block())

    def wblock(w, r, c):
        return w[r * B:(r + 1) * B, c * B:(c + 1) * B].rearrange("(k p) n -> p k n", p=P)

    def step_units(w1, w3, w2, s):
        up = [wblock(w1, 0, s), wblock(w1, 1, s), wblock(w3, 0, s), wblock(w3, 1, s)] if s < NSTEP else []
        return up + ([wblock(w2, s - 1, 0), wblock(w2, s - 1, 1)] if s else [])

    def dyn_units(w1, w3, w2, s):
        def blk(w, r):
            return w[r * B:(r + 1) * B, bass.ts(s, B)].rearrange("(k p) n -> p k n", p=P)
        down = w2[bass.ts(s - 1, B), :]
        return [blk(w1, 0), blk(w1, 1), blk(w3, 0), blk(w3, 1)] + [
            down[:, c * B:(c + 1) * B].rearrange("(k p) n -> p k n", p=P) for c in range(2)]

    @block.sync
    def _(sp):
        def load(u, src):
            if u >= RAW:
                plain, n = kind(u - RAW)
                sp.wait_ge(plain_used if plain else lo_ready, n + 1)
            sp.dma_start(raw[:, u % RAW], src).then_inc(raw_in[u % RAW], 16)

        def load_ada(l):
            for c in range(N_ADA // 2):
                for r in range(2):
                    load(U_ADA[l] + 2 * c + r, wblock(d['ada_w'][l], r, c))

        def load_in(l):
            for c in range(3):
                for r in range(2):
                    load(U_IN[l] + 2 * c + r, wblock(d['w_in'][l], r, c))

        def load_out(l):
            for c in range(2):
                for r in range(2):
                    load(U_OUT[l] + 2 * c + r, wblock(d['w_out'][l], r, c))

        load_ada(0)
        load_in(0)
        load_ada(1)
        load_out(0)
        w = (d['ffn_w1'][0], d['ffn_w3'][0], d['ffn_w2'][0])
        for j, src in enumerate(step_units(*w, 0)):
            load(U_FFN + j, src)
        with sp.Fori(1, NSTEP) as s:
            for j, src in enumerate(dyn_units(*w, s)):
                sp.wait_ge(lo_ready, s * 6 + (S_FFN + 4 - 6 + j - RAW + 1))
                slot = (U_FFN + 4 + j) % RAW
                sp.dma_start(raw[:, slot], src).then_inc(raw_in[slot], 16)
        for j, src in enumerate(step_units(*w, NSTEP)):
            load(U_FFN + 4 + 6 * (NSTEP - 1) + j, src)
        load_in(1)
        load_out(1)

        def load_item(i, e):
            w = (d['moe_w1'][0, e], d['moe_w3'][0, e], d['moe_w2'][0, e])

            def put(j, src, s=None):
                n = i * N_FFN + (S_MOE + j - RAW + 1)
                sp.wait_ge(lo_ready, n if s is None else n + s * 6)
                slot = (U_MOE + j) % RAW
                sp.dma_start(raw[:, slot], src).then_inc(raw_in[slot], 16)

            for j, src in enumerate(step_units(*w, 0)):
                put(j, src)
            with sp.Fori(1, NSTEP) as s:
                for j, src in enumerate(dyn_units(*w, s)):
                    put(4 - 6 + j, src, s)
            for j, src in enumerate(step_units(*w, NSTEP)):
                put(4 + 6 * (NSTEP - 1) + j, src)

        with sp.Fori(0, E) as e:
            load_item(e, e)
        sp.wait_ge(routed, 1)
        n_items = sp.value_load(table[0:1, EXTRA_MAX:EXTRA_MAX + 1], min_val=E, max_val=E + EXTRA_MAX)
        with sp.If(n_items > E):
            with sp.Fori(E, n_items) as i:
                ex = sp.value_load(table[0:1, bass.ds(i - E, 1)], min_val=0, max_val=E - 1)
                load_item(i, ex)
            sp.nop()
        for b in range(NBLK):
            n = BLK[b]
            sp.wait_ge(fin_cp, b + 1)
            dst = o[0][0, b * P:(b + 1) * P, :] if b < 2 else o[1].rearrange("b t d -> (b t) d")
            sp.dma_start(dst, xtok[0:n, b, :]).then_inc(y_stored, 16)
        sp.wait_ge(y_stored, 16 * NBLK)
        sp.wait_ge(stored, 16 * DEPTH * 3)
        sp.wait_ge(v_stored, 16 * DEPTH * 2)

    @block.gpsimd
    def _(gp):
        steps = [0]

        def step(ins):
            steps[0] += 1
            ins.then_inc(pool_step, 1)
            gp.wait_ge(pool_step, steps[0])

        def load_layer(l):
            gp.dma_start(pw[:], d['pool_w'][l].rearrange("g c e -> c g e")).then_inc(layer_in, 16)
            gp.dma_start(g_bias, d['sgu_b'][l:l + 1]).then_inc(layer_in, 16)
            gp.dma_start(vng[:], d['v_norm_g'][l].partition_broadcast(P)).then_inc(layer_in, 16)
            gp.dma_start(vnb[:], d['v_norm_b'][l].partition_broadcast(P)).then_inc(layer_in, 16)

        g = nc.gpsimd
        step(g.memset(ident[:], 0.0))
        step(g.affine_select(out=ident[:], in_=ident[:], compare_op=ALU.not_equal, fill=1.0, base=0,
                             pattern=[[-1, P]], channel_multiplier=1))
        step(g.memset(ones[:], 1.0))
        step(g.memset(gs_raw, 0.0))
        g.memset(eps[:], EPS).then_inc(const, 1)
        for b in range(NSEQ):
            for l in range(DEPTH):
                gp.dma_start(gs_raw[b * TS:(b + 1) * TS, l * H:(l + 1) * H, NS_TOK + b * TS:NS_TOK + (b + 1) * TS],
                             d['sgu_w'][l, :, 0:TS, 0:TS].rearrange("h t s -> t h s")).then_inc(aux_in, 16)
        gp.dma_start(buf_raw[0:NSEQ * BUF], d['state_pool'].rearrange("l b r c -> (b r) l c")).then_inc(aux_in, 16)
        load_layer(0)
        for l in range(DEPTH):
            gp.dma_start(o[3][l, :, 0:BUF - TS, :], d['state_pool'][l, :, TS:BUF, :]).then_inc(stored, 16)
        g.affine_select(out=below[:], in_=ones[:], compare_op=ALU.is_gt, fill=0.0, base=0,
                        pattern=[[1, P]], channel_multiplier=-1)
        step(g.iota(iota_i[:], pattern=[[1, P]], base=0, channel_multiplier=0))
        step(g.tensor_copy(iota[:], iota_i[:]))
        g.memset(pp[:, :, 0:PADP], 0.0)
        g.memset(logit[:], 0.0).then_inc(zeroed, 1)
        gp.wait_ge(prep_cp, 4)
        step(g.affine_select(out=gw[:], in_=gw[:], compare_op=ALU.is_ge, fill=0.0, base=0,
                             pattern=[[0, DEPTH * H], [1, P]], channel_multiplier=-1))
        g.affine_select(out=gs[:], in_=gs[:], compare_op=ALU.is_ge, fill=0.0, base=P - NS_TOK,
                        pattern=[[0, DEPTH * H], [1, NS_TOK]], channel_multiplier=-1).then_inc(masked, 1)

        for l in range(DEPTH):
            gp.wait_ge(p_out, 2 * (l + 1))
            n = PADP + NP_TOK
            src, ssrc = pp, sp_[:, l]
            for j, w in enumerate(WIN):
                dst, sdst = (wa, wsa) if j % 2 == 0 else (wb, wsb)
                half, lo, slo = w // 2, PADP - (16 - w), w - 1
                g.tensor_tensor(dst[:, j:, lo:n], src[:, j:, lo:n], src[:, j:, lo - half:n - half], ALU.add)
                ins = g.tensor_tensor(sdst[:, j:, :, slo:], ssrc[:, j:, :, slo:],
                                      ssrc[:, j:, :, slo - half:BUF + TS - half], ALU.add)
                step(ins)
                src, ssrc = dst, sdst
            g.nop().then_inc(win_s, 1)
            gp.wait_ge(v_done, l + 1)
            gp.dma_start(o[4][l, 0], v_norm[:, 1, :]).then_inc(v_stored, 16)
            gp.dma_start(o[5][l].rearrange("b t c -> (b t) c"), v_norm[NS_TOK:P, 2, :]).then_inc(v_stored, 16)
            gp.wait_ge(st_cp, l + 1)
            gp.dma_start(o[2][l, 0], pst[NS_TOK:NS_TOK + BUF]).then_inc(stored, 16)
            gp.dma_start(o[3][l, :, BUF - TS:, :], pst[0:NS_TOK]).then_inc(stored, 16)
            if l + 1 < DEPTH:
                gp.wait_ge(gate_mm, l + 1)
                gp.wait_ge(pool_mm, H * (l + 1))
                load_layer(l + 1)

    @block.scalar
    def _(act):
        a = nc.scalar
        cur = [0]

        def hi(s, n=None):
            u = unit_of_split(s)
            act.wait_ge(raw_in[u % RAW], 16 * (u // RAW + 1))
            if s >= SPL:
                act.wait_ge(split_used, s - SPL + 1)
            a.activation(w_hi[:, s % SPL], raw[:, u % RAW], ACT.Copy).then_inc(hi_ready, 1)

        def hi_loop(u0, s0, j, t, per):
            act.wait_ge(raw_in[(u0 + j) % RAW], t * 16 + 16 * ((u0 + j) // RAW + 1))
            act.wait_ge(split_used, per + (s0 + j - SPL + 1))
            a.activation(w_hi[:, (s0 + j) % SPL], raw[:, (u0 + j) % RAW], ACT.Copy).then_inc(hi_ready, 1)

        def hi_to(s):
            while cur[0] < s:
                hi(cur[0])
                cur[0] += 1

        act.dma_start(crow[0:1, :], d['c_prompt']).then_inc(c_in, 16)
        act.dma_start(crow[1:ROWS, :], d['c_sample']).then_inc(c_in, 16)
        for r, name in ((R_N1, 'norm1_g'), (R_N2, 'norm2_g'), (R_ADAB, 'ada_b'), (R_PS, 'pool_scale'),
                        (R_AG, 'branch_a_g'), (R_BG, 'branch_b_g')):
            n = d[name].shape[1] // P
            act.dma_start(vrow[r:r + n], d[name].rearrange("l (j p) -> j l p", p=P)).then_inc(vec_in, 16)
        for l in range(DEPTH):
            act.dma_start(vrow[R_FG:R_FG + KD, l, :], d['final_g'].rearrange("(j p) -> j p", p=P)).then_inc(vec_in, 16)
        for b in range(2):
            act.dma_start(xtok[:, b, :], d['x_prompt'][0, b * P:(b + 1) * P, :]).then_inc(x_in, 16)
        act.dma_start(xtok[0:NS_TOK, 2, :], d['x_sample'].rearrange("b t d -> (b t) d")).then_inc(x_in, 16)
        act.dma_start(gw_raw, d['sgu_w'].rearrange("l h t s -> t (l h) s")).then_inc(gw_in, 16)
        act.dma_start(rw[:], d['router_w'][0].rearrange("(k p) e -> p k e", p=P)).then_inc(rw_in, 16)
        act.wait_ge(c_in, 16 * N_C)
        a.activation(cs_row[:], crow[:], ACT.Silu).then_inc(act_c, 1)

        def ada(l, c):
            n = 12 * l + c
            act.wait_ge(plain_used, 2 * n + 2)
            if n >= 1:
                act.wait_ge(row_tr, n)
            a.activation(modrow[:], ps[0:ROWS, 6 + c % 2, :], ACT.Copy).then_inc(row_out, 1)

        def square(n0, src, k0, k1, wait):
            for k in range(k0, k1, 2):
                wait(k)
                a.activation(sq[:, k:k + 2, :], src(k), ACT.Square).then_inc(sq_ready, 1)

        def std(n, bank, width):
            act.wait_ge(ssum, n + 1)
            a.activation(stdt[:], ps[:, bank, 0:T], ACT.Sqrt, scale=1.0 / width, bias=eps[:]).then_inc(std_ready, 1)

        def norm(l, which):
            n = 2 * l + which
            for k in range(0, KD, 2):
                if n:
                    act.wait_ge(x_new, 4 * (n - 1) + k // 2 + 1)
                else:
                    act.wait_ge(x_cp, k + 2)
                a.activation(sq[:, k:k + 2, :], x[:, k:k + 2, :], ACT.Square).then_inc(sq_ready, 1)
            std(4 * l + 3 * which, 0, D)
            for b in range(KD // 2 + 1):
                if b < KD // 2:
                    act.wait_ge(scaled, 4 * n + b + 1)
                    for k in (2 * b, 2 * b + 1):
                        a.activation(hf[:, k, 0:NP_TOK], hf[:, k, 0:NP_TOK], ACT.Identity,
                                     scale=gain[:, l, which, k, 0:1],
                                     bias=mod[:, l, 3 * KD * which + k, 0:1]).then_inc(affine, 1)
                if b >= 1 and n < 3:
                    act.wait_ge(affine, 8 * n + 2 * b)
                    a.activation(h_hi[:, 2 * b - 2:2 * b, 0:T], hf[:, 2 * b - 2:2 * b, :], ACT.Copy).then_inc(hhi, 1)

        def project_in(l):
            s = S_IN[l]
            hi_to(s + 3)
            act.wait_ge(split_used, s + 2)
            if l:
                act.wait_ge(h_ready, 12 * l)
            a.activation(uT[:], ps[:, 0:H, 0:T], ACT.Gelu_apprx_tanh).then_inc(u_out, 1)
            hi_to(s + 5)
            act.wait_ge(split_used, s + 4)
            a.activation(v_gelu[:], ps[:, 4:4 + NBLK, :], ACT.Gelu_apprx_tanh).then_inc(v_out, 1)
            hi_to(s + 6)
            act.wait_ge(v_var, l + 1)
            a.activation(v_std[:], v_mv[:, :, 1], ACT.Sqrt, bias=eps[:]).then_inc(v_sd, 1)
            act.wait_ge(split_used, s + 6)
            a.activation(pp[:, :, PADP:], ps[:, 0:H, 0:NP_TOK], ACT.Copy).then_inc(p_out, 1)
            for gi in range(H):
                a.activation(sp_[:, l, gi, :, BUF:], ps[:, gi, NP_TOK:T].rearrange("p (b t) -> p b t", t=TS),
                             ACT.Copy)
            a.activation(sps, ps[:, 0:H, NP_TOK:T], ACT.Copy).then_inc(p_out, 1)
            act.wait_ge(st_tr, l + 1)
            if l:
                act.wait_ge(stored, 16 * (2 + 2 * l))
            a.activation(pst[NS_TOK:NS_TOK + BUF], ps[0:BUF, 3, :], ACT.Copy)
            a.activation(pst[0:NS_TOK], ps[0:NS_TOK, 4, :], ACT.Copy).then_inc(st_cp, 1)

        def mix_pool(l):
            act.wait_ge(v_done, l + 1)
            for gi in range(H):
                act.wait_ge(pool_mm, H * l + gi + 1)
                a.activation(yb[:, gi, :], ps[:, 4, 0:T], ACT.Copy,
                             scale=vec[:, l, R_PS + gi:R_PS + gi + 1]).then_inc(yb_done, 1)
            for k in range(0, H, 2):
                act.wait_ge(yb_done, H * l + k + 2)
                a.activation(sq[:, H + k:H + k + 2, :], yb[:, k:k + 2, :], ACT.Square).then_inc(sq_ready, 1)
            std(4 * l + 1, 4, HALF)
            for k in range(0, H, 2):
                act.wait_ge(mixed, 4 * l + k // 2 + 1)
                a.activation(h_hi[:, H + k:H + k + 2, 0:T], hf[:, H + k:H + k + 2, :], ACT.Copy).then_inc(mixed_hi, 1)

        def mix_gate(l):
            act.wait_ge(ya_done, l + 1)
            for k in range(0, H, 2):
                a.activation(sq[:, k:k + 2, :], uT[:, k:k + 2, :], ACT.Square).then_inc(sq_ready, 1)
            std(4 * l + 2, 0, HALF)
            for k in range(0, H, 2):
                act.wait_ge(mixed, 4 * l + 2 + k // 2 + 1)
                a.activation(h_hi[:, k:k + 2, 0:T], hf[:, k:k + 2, :], ACT.Copy).then_inc(mixed_hi, 1)

        for c in range(12):
            ada(0, c)
        norm(0, 0)
        project_in(0)
        ada(1, 0)
        ada(1, 1)
        ada(1, 2)
        mix_gate_pool = (mix_pool, mix_gate)
        mix_gate_pool[0](0)
        for c in range(3, 6):
            ada(1, c)
        mix_gate_pool[1](0)
        for c in range(6, 12):
            ada(1, c)
        hi_to(S_OUT[0] + N_OUT)
        norm(0, 1)

        def ffn_silu(n):
            act.wait_ge(split_used, n[0])
            a.activation(silu_t[:], ps[:, 0:KB, 0:T], ACT.Silu).then_inc(f_silu, 1)

        def ffn_hi(used, mul):
            act.wait_ge(split_used, used)
            act.wait_ge(f_mul, mul)
            a.activation(g_hi[:], g_f[:], ACT.Copy).then_inc(f_hi, 1)

        s0 = S_FFN
        hi_to(s0 + 4)
        ffn_silu([s0 + 2])
        hi_to(s0 + 6)
        ffn_hi(s0 + 4, 1)
        u1, s1 = U_FFN + 4, S_FFN + 4
        with act.Fori(1, NSTEP - 1) as s:
            t = s - 1
            hi_loop(u1, s1, 2, t, t * 6)
            hi_loop(u1, s1, 3, t, t * 6)
            act.wait_ge(f_lo, s)
            ffn_silu([t * 6 + (s1 + 2)])
            for j in range(4, 8):
                hi_loop(u1, s1, j, t, t * 6)
            ffn_hi(t * 6 + (s1 + 6), s + 1)
        cur[0] = s1 + 6 * 5 + 2
        hi_to(cur[0] + 2)
        act.wait_ge(f_lo, 6)
        ffn_silu([s1 + 32])
        hi_to(cur[0] + 2)
        hi_to(cur[0] + 2)
        ffn_hi(s1 + 36, 7)
        norm(1, 0)
        project_in(1)
        mix_pool(1)
        mix_gate(1)
        hi_to(S_OUT[1] + N_OUT)
        norm(1, 1)

        for b in range(NBLK):
            n = BLK[b]
            act.wait_ge(tok_tr, b + 1)
            a.activation(ht_hi[0:n, b, :], ps[0:n, 2 + 2 * b:4 + 2 * b, :].rearrange("p a c -> p (a c)"),
                         ACT.Copy).then_inc(tok_hi, 1)
        act.wait_ge(top_done, 1)
        a.activation(etop[:], dtop[:], ACT.Exp).then_inc(exp_done, 1)

        def gather_hi(n):
            act.wait_ge(gath, n)
            a.activation(xs_hi[:], ps[:, 5:7, :].rearrange("p a (b c) -> p (a b) c", c=P), ACT.Copy).then_inc(xhi, 1)

        gather_hi(1)
        hi_to(S_MOE)
        act.wait_ge(routed, 1)
        n_items = act.value_load(table[0:1, EXTRA_MAX:EXTRA_MAX + 1], min_val=E, max_val=E + EXTRA_MAX)

        with act.Fori(0, n_items) as i:
            def e_up(j, s=None):
                k = i * N_FFN if s is None else i * N_FFN + s * 6
                turn = i * (N_FFN // RAW) if s is None else i * (N_FFN // RAW) + s
                hi_loop(U_MOE, S_MOE, j, turn, k)

            def e_silu_step(s):
                act.wait_ge(split_used, i * N_FFN + (S_MOE + 2) if s is None else i * N_FFN + s * 6 + (S_MOE - 2 + 2))
                if s is not None:
                    act.wait_ge(e_mu, i * NSTEP + s)
                a.activation(e_silu[:], ps[:, 0, :], ACT.Silu).then_inc(e_si, 1)

            def gt_split(n):
                act.wait_ge(e_tr, n)
                a.activation(gt_hi[:], ps[:, 2, :].rearrange("p (a b) -> p a b", b=P), ACT.Copy).then_inc(e_hi, 1)

            for j in range(4):
                e_up(j)
            act.wait_ge(gat_step, i * 2 + 1)
            e_silu_step(None)
            with act.Fori(1, NSTEP) as s:
                for j in range(4):
                    e_up(j - 2, s)
                gt_split(i * NSTEP + s)
                for j in range(4, 6):
                    e_up(j - 2, s)
                e_silu_step(s)
            gather_hi(i + 2)
            gt_split(i * NSTEP + NSTEP)
            act.wait_ge(gat_tr, i + 1)
            a.activation(gatT[:], ps[:, 1, 0:T], ACT.Copy).then_inc(gat_cp, 1)
            for j in range(2):
                e_up(4 + 6 * 6 + j)
            act.wait_ge(split_used, i * N_FFN + (S_MOE + N_FFN))
            a.activation(e_y[:], ps[:, 3:5, :].rearrange("p a c -> p (a c)"), ACT.Copy).then_inc(y_cp, 1)

        for k in range(0, KD, 2):
            act.wait_ge(x_new, 12 + k // 2 + 1)
            a.activation(sq[:, k:k + 2, :], x[:, k:k + 2, :], ACT.Square).then_inc(sq_ready, 1)
        std(8, 0, D)
        act.wait_ge(v_stored, 32 * DEPTH)
        for b in range(NBLK):
            n = BLK[b]
            act.wait_ge(fin_tr, b + 1)
            a.activation(xtok[0:n, b, :], ps[0:n, 2 + 2 * b:4 + 2 * b, :].rearrange("p a c -> p (a c)"),
                         ACT.Copy).then_inc(fin_cp, 1)

    @block.vector
    def _(ve):
        v = nc.vector
        steps = [0]
        cur = [0]

        def step(ins):
            steps[0] += 1
            ins.then_inc(dve, 1)
            ve.wait_ge(dve, steps[0])

        def lo(s):
            u = unit_of_split(s)
            ve.wait_ge(hi_ready, s + 1)
            v.tensor_tensor(w_lo[:, s % SPL], raw[:, u % RAW], w_hi[:, s % SPL].bitcast(F32),
                            ALU.subtract).then_inc(lo_ready, 1)

        def lo_loop(u0, s0, j, per):
            ve.wait_ge(hi_ready, per + (s0 + j + 1))
            v.tensor_tensor(w_lo[:, (s0 + j) % SPL], raw[:, (u0 + j) % RAW], w_hi[:, (s0 + j) % SPL].bitcast(F32),
                            ALU.subtract).then_inc(lo_ready, 1)

        def lo_to(s):
            while cur[0] < s:
                lo(cur[0])
                cur[0] += 1

        ve.wait_ge(prep_tr, 1)
        v.tensor_copy(cT[:], ps[:, 0, 0:KD * ROWS].rearrange("p (k r) -> p k r", r=ROWS)).then_inc(prep_cp, 1)
        ve.wait_ge(prep_tr, 2)
        v.tensor_copy(vec[:], ps[:, 1, 0:DEPTH * NV].rearrange("p (l n) -> p l n", n=NV)).then_inc(prep_cp, 1)
        for k in range(KD):
            ve.wait_ge(prep_tr, 3 + k)
            v.tensor_copy(x[:, k, :], ps[:, 2 + k % 2, 0:T]).then_inc(x_cp, 1)
        for l in range(DEPTH):
            ve.wait_ge(prep_tr, 11 + l)
            v.tensor_copy(gw[:, l], ps[:, 4, :].rearrange("p (h t) -> p h t", t=P))
            v.tensor_copy(gs[:, l], ps[:, 5, 0:H * NS_TOK].rearrange("p (h t) -> p h t", t=NS_TOK)
                          ).then_inc(prep_cp, 1)
        for l in range(DEPTH):
            ve.wait_ge(prep_tr, 13 + l)
            v.tensor_copy(sp_[:, l, :, :, 0:BUF],
                          ps[:, 4, 0:H * NSEQ * BUF].rearrange("p (g b r) -> p g b r", g=H, r=BUF)).then_inc(prep_cp, 1)
        ve.wait_ge(const, 1)
        ve.wait_ge(zeroed, 1)
        for gi, w in enumerate(WIN):
            ins = v.tensor_scalar(first[:, gi, :], iota[:, 0:PADP], 1.0, float(w), ALU.add, ALU.min)
        step(ins)
        step(v.reciprocal(rcnt[:], first[:]))

        def ada_add(l, c):
            n = 12 * l + c
            ve.wait_ge(row_tr, n + 1)
            v.tensor_tensor(mod[:, l, 4 * c:4 * c + 4, :],
                            ps[:, 5, 0:4 * ROWS].rearrange("p (m r) -> p m r", r=ROWS),
                            vec[:, l, R_ADAB + 4 * c:R_ADAB + 4 * c + 4].unsqueeze(2).to_broadcast([P, 4, ROWS]),
                            ALU.add).then_inc(mod_add, 1)

        def ada_gain(l):
            ve.wait_ge(mod_add, 12 * (l + 1))
            for which, r in ((0, R_N1), (1, R_N2)):
                c = (3 * which + 1) * KD
                ins = v.scalar_tensor_tensor(out=gain[:, l, which], in0=mod[:, l, c:c + KD, :], scalar=1.0,
                                             in1=vec[:, l, r:r + KD].unsqueeze(2).to_broadcast([P, KD, ROWS]),
                                             op0=ALU.add, op1=ALU.mult)
            ins.then_inc(mod_ready, 1)
            ve.wait_ge(mod_ready, l + 1)

        def norm(l, which):
            n = 2 * l + which
            ve.wait_ge(std_ready, 4 * l + 3 * which + 1)
            step(v.reciprocal(rstd[:], stdt[:]))

            def scale_pair(b):
                k = 2 * b
                step(v.tensor_tensor(hf[:, k:k + 2, :], x[:, k:k + 2, :],
                                     rstd[:].unsqueeze(1).to_broadcast([P, 2, T]), ALU.mult))
                smp_v = hf[:, k:k + 2, NP_TOK:T].rearrange("p k (b t) -> p k b t", t=TS)
                gn = gain[:, l, which, k:k + 2, 1:ROWS].unsqueeze(3).to_broadcast([P, 2, NSEQ, TS])
                sh = mod[:, l, 3 * KD * which + k:3 * KD * which + k + 2, 1:ROWS].unsqueeze(3).to_broadcast(
                    [P, 2, NSEQ, TS])
                step(v.tensor_tensor(smp_v, smp_v, gn, ALU.mult))
                v.tensor_tensor(smp_v, smp_v, sh, ALU.add).then_inc(scaled, 1)

            for b in range(KD // 2 + 1):
                if b < KD // 2:
                    scale_pair(b)
                if b >= 1 and n < 3:
                    k = 2 * b - 2
                    ve.wait_ge(hhi, 4 * n + b)
                    ve.wait_ge(scaled, 4 * n + b)
                    v.tensor_tensor(h_lo[:, k:k + 2, 0:T], hf[:, k:k + 2, :], h_hi[:, k:k + 2, 0:T].bitcast(F32),
                                    ALU.subtract).then_inc(h_ready, 1)

        def project_in(l):
            s = S_IN[l]
            lo_to(s + 5)
            ve.wait_ge(v_out, l + 1)
            if l:
                ve.wait_ge(v_stored, 32 * l)
            for j in range(NBLK * H):
                ins = v.bn_stats(v_stat[:, j, :], v_gelu[:, j // H, (j % H) * P:(j % H + 1) * P])
            step(ins)
            for j in range(NBLK * H):
                ins = v.bn_aggr(v_mv[:, j, :], v_stat[:, j, :])
            ins.then_inc(v_var, 1)
            lo_to(s + 6)
            ve.wait_ge(v_sd, l + 1)
            ve.wait_ge(layer_in, 64 * (l + 1))
            ve.wait_ge(v_var, l + 1)
            step(v.reciprocal(v_rstd[:], v_std[:]))
            for j in range(NBLK * H):
                cols = slice((j % H) * P, (j % H + 1) * P)
                ins = v.tensor_scalar(v_norm[:, j // H, cols], v_gelu[:, j // H, cols], v_mv[:, j, 0:1],
                                      v_rstd[:, j:j + 1], ALU.subtract, ALU.mult)
            step(ins)
            step(v.tensor_tensor(v_norm[:], v_norm[:], vng[:].unsqueeze(1).to_broadcast([P, NBLK, HALF]),
                                 ALU.mult))
            v.tensor_tensor(v_norm[:], v_norm[:], vnb[:].unsqueeze(1).to_broadcast([P, NBLK, HALF]),
                            ALU.add).then_inc(v_done, 1)

        def pooled(l):
            ve.wait_ge(win_s, l + 1)
            for j, w in enumerate(WIN):
                ws, wss = (wa, wsa) if j % 2 == 0 else (wb, wsb)
                dj, djs = (wb, wsb) if j % 2 == 0 else (wa, wsa)
                v.scalar_tensor_tensor(out=dj[:, j, 2 * PADP:], in0=ws[:, j, 2 * PADP:], scalar=1.0 / w,
                                       in1=pp[:, j, 2 * PADP:], op0=ALU.mult, op1=ALU.subtract)
                v.scalar_tensor_tensor(out=djs[:, j, :, BUF:], in0=wss[:, j, :, BUF:], scalar=1.0 / w,
                                       in1=sp_[:, l, j, :, BUF:], op0=ALU.mult, op1=ALU.subtract)
                ins = v.tensor_tensor(first[:, j, :], ws[:, j, PADP:2 * PADP], rcnt[:, j, :], ALU.mult)
            step(ins)
            for j in range(H):
                dj = wb if j % 2 == 0 else wa
                ins = v.tensor_tensor(dj[:, j, PADP:2 * PADP], first[:, j, :], pp[:, j, PADP:2 * PADP], ALU.subtract)
            ins.then_inc(d_done, 1)

        def branch(l, n_std, src, k0, row, n_mix):
            ve.wait_ge(std_ready, n_std)
            step(v.reciprocal(rstd[:], stdt[:]))
            for k in range(H):
                ins = v.scalar_tensor_tensor(out=hf[:, k0 + k, :], in0=src[:, k, :],
                                             scalar=vec[:, l, row + k:row + k + 1], in1=rstd[:],
                                             op0=ALU.mult, op1=ALU.mult)
                if k % 2:
                    ins.then_inc(mixed, 1)
            for k in range(0, H, 2):
                ve.wait_ge(mixed_hi, n_mix + k // 2 + 1)
                v.tensor_tensor(h_lo[:, k0 + k:k0 + k + 2, 0:T], hf[:, k0 + k:k0 + k + 2, :],
                                h_hi[:, k0 + k:k0 + k + 2, 0:T].bitcast(F32), ALU.subtract).then_inc(h_ready, 1)

        def mix_pool(l):
            branch(l, 4 * l + 2, yb, H, R_BG, 4 * l)

        def mix_gate(l):
            ve.wait_ge(gate_mm, l + 1)
            v.tensor_tensor(uT[:], uT[:], ps[:, 0:H, 0:T], ALU.mult).then_inc(ya_done, 1)
            branch(l, 4 * l + 3, uT, 0, R_AG, 4 * l + 2)

        pairs = [0]

        def residual(l, mod_chunk, k, src):
            gt = mod[:, l, mod_chunk + k:mod_chunk + k + 2, :]
            for q in range(2):
                v.scalar_tensor_tensor(out=x[:, k + q, 0:NP_TOK], in0=src[:, q, 0:NP_TOK], scalar=gt[:, q, 0:1],
                                       in1=x[:, k + q, 0:NP_TOK], op0=ALU.mult, op1=ALU.add)
            if pairs[0]:
                ve.wait_ge(x_new, pairs[0])
            step(v.tensor_tensor(smp[:].rearrange("p k (b t) -> p k b t", t=TS),
                                 src[:, :, NP_TOK:T].rearrange("p k (b t) -> p k b t", t=TS),
                                 gt[:, :, 1:ROWS].unsqueeze(3).to_broadcast([P, 2, NSEQ, TS]), ALU.mult))
            v.tensor_tensor(x[:, k:k + 2, NP_TOK:T], x[:, k:k + 2, NP_TOK:T], smp[:], ALU.add).then_inc(x_new, 1)
            pairs[0] += 1

        def project_out(l):
            s = S_OUT[l]
            lo_to(s + 4)
            for c in range(2):
                ve.wait_ge(split_used, s + 2 * c + 2)
                for m in (0, 2):
                    residual(l, 2 * KD, 4 * c + m, ps[:, 4 * c + m:4 * c + m + 2, :])

        for c in range(12):
            ada_add(0, c)
        ada_gain(0)
        norm(0, 0)
        project_in(0)
        ada_add(1, 0)
        ada_add(1, 1)
        pooled(0)
        ada_add(1, 2)
        mix_pool(0)
        for c in range(3, 5):
            ada_add(1, c)
        mix_gate(0)
        for c in range(5, 12):
            ada_add(1, c)
        ada_gain(1)
        project_out(0)
        norm(0, 1)

        def ffn_mul(used, n):
            ve.wait_ge(split_used, used)
            ve.wait_ge(f_silu, n)
            v.tensor_tensor(g_f[:], silu_t[:], ps[:, KB:2 * KB, 0:T], ALU.mult).then_inc(f_mul, 1)

        def ffn_lo(n):
            ve.wait_ge(f_hi, n)
            ve.wait_ge(f_mul, n)
            v.tensor_tensor(g_lo[:], g_f[:], g_hi[:].bitcast(F32), ALU.subtract).then_inc(f_lo, 1)

        def ffn_add(c, used, own):
            ve.wait_ge(split_used, used)
            ve.wait_ge(f_add, own)
            half = facc[:, 4 * c:4 * c + 4, :]
            v.tensor_tensor(half, half, ps[:, 4 * c:4 * c + 4, 0:T], ALU.add).then_inc(f_add, 1)

        s0, s1, u1 = S_FFN, S_FFN + 4, U_FFN + 4
        v.memset(facc[:], 0.0).then_inc(f_add, 1)
        lo_to(s0 + 4)
        ffn_mul(s0 + 4, 1)
        lo_to(s0 + 6)
        ffn_lo(1)
        with ve.Fori(1, NSTEP - 1) as s:
            per = (s - 1) * 6
            for j in range(2, 6):
                lo_loop(u1, s1, j, per)
            ffn_mul(per + (s1 + 4), s + 1)
            ffn_add(0, per + (s1 + 5), s * 2 - 1)
            lo_loop(u1, s1, 6, per)
            lo_loop(u1, s1, 7, per)
            ffn_add(1, per + (s1 + 6), s * 2)
            ffn_lo(s + 1)
        cur[0] = s1 + 6 * 5 + 2
        lo_to(cur[0] + 4)
        ffn_mul(s1 + 34, 7)
        ffn_add(0, s1 + 35, 11)
        ffn_add(1, s1 + 36, 12)
        lo_to(cur[0] + 2)
        ffn_lo(7)
        ffn_add(0, s1 + 37, 13)
        ffn_add(1, s1 + 38, 14)
        ve.wait_ge(f_add, 15)
        for k in range(0, KD, 2):
            residual(0, 5 * KD, k, facc[:, k:k + 2, :])

        norm(1, 0)
        project_in(1)
        pooled(1)
        mix_pool(1)
        mix_gate(1)
        project_out(1)
        norm(1, 1)

        for b in range(NBLK):
            n = BLK[b]
            ve.wait_ge(log_mm, 1)
            ins = v.tensor_copy(logit[0:n, b, :], ps[0:n, 0, b * E:(b + 1) * E])
        step(ins)
        for b in range(NBLK):
            ins = v.max(top[:, b, :], logit[:, b, :])
        step(ins)
        for b in range(NBLK):
            ins = v.max_index(topi[:, b, :], top[:, b, :], logit[:, b, :])
        step(v.tensor_tensor(dtop[:], top[:, :, 1], top[:, :, 0], ALU.subtract))
        v.nop().then_inc(top_done, 1)
        step(v.tensor_copy(topf[:], topi[:]))
        for j in range(2):
            ins = v.tensor_tensor(oh[:, j], iota[:, 0:E].unsqueeze(1).to_broadcast([P, NBLK, E]),
                                  topf[:, :, j].unsqueeze(2).to_broadcast([P, NBLK, E]), ALU.is_equal)
        step(ins)
        v.tensor_tensor(chosen[:], oh[:, 0], oh[:, 1], ALU.add).then_inc(chosen_r, 1)
        for b in range(NBLK):
            n = BLK[b]
            ve.wait_ge(tok_hi, b + 1)
            v.tensor_tensor(ht_lo[0:n, b, :], ps[0:n, 2 + 2 * b:4 + 2 * b, :].rearrange("p a c -> p (a c)"),
                            ht_hi[0:n, b, :].bitcast(F32), ALU.subtract).then_inc(tok_lo, 1)
        ve.wait_ge(exp_done, 1)
        step(v.tensor_scalar(dsum[:], etop[:], 1.0, None, ALU.add))
        step(v.reciprocal(gate[:, 0], dsum[:]))
        v.tensor_tensor(gate[:, 1], etop[:], gate[:, 0], ALU.mult)
        ve.wait_ge(rank_mm, 1)
        v.memset(rank[:], 0.0)
        step(v.tensor_copy(cnt[:], ps[:, 1, NBLK * E:NBLK * E + E]))
        for b in range(NBLK):
            n = BLK[b]
            ins = v.tensor_copy(rank[0:n, b, :], ps[0:n, 1, b * E:(b + 1) * E])
        step(ins)
        v.tensor_scalar(ext[:], cnt[:], float(P), None, ALU.is_gt)
        step(v.tensor_scalar(ext2[:], cnt[:], float(2 * P), None, ALU.is_gt))
        step(v.tensor_tensor(ext[:], ext[:], ext2[:], ALU.add))
        step(v.memset(ebase[:], 0.0))
        for e in range(1, E):
            step(v.tensor_tensor(ebase[:, e:e + 1], ebase[:, e - 1:e], ext[:, e - 1:e], ALU.add))
        step(v.tensor_tensor(eoff[:], ebase[:], iota[:, 0:E], ALU.subtract))
        step(v.tensor_scalar(eoff[:], eoff[:], float(E - 1), float(P), ALU.add, ALU.mult))
        v.tensor_scalar(over1[:], rank[:], float(P), None, ALU.is_ge)
        step(v.tensor_scalar(posn[:], iota[:, 0:E].unsqueeze(1).to_broadcast([P, NBLK, E]), float(P), None,
                             ALU.mult))
        step(v.tensor_tensor(posn[:], posn[:], rank[:], ALU.add))
        step(v.tensor_tensor(over1[:], over1[:], eoff[:].unsqueeze(1).to_broadcast([P, NBLK, E]), ALU.mult))
        step(v.tensor_tensor(posn[:], posn[:], over1[:], ALU.add))
        for j in range(2):
            step(v.tensor_tensor(tmpe[:], oh[:, j], posn[:], ALU.mult))
            step(v.tensor_reduce(pos[:, j], tmpe[:], AX.X, ALU.add))
        step(v.memset(tab[:], 0.0))
        step(v.tensor_tensor(ext2[:], ebase[:], ext[:], ALU.add))
        for j in range(EXTRA_MAX):
            v.tensor_scalar(inj[:], ebase[:], float(j), None, ALU.is_le)
            step(v.tensor_scalar(inj2[:], ext2[:], float(j), None, ALU.is_gt))
            step(v.tensor_tensor(inj[:], inj[:], inj2[:], ALU.mult))
            step(v.tensor_tensor(inj[:], inj[:], iota[:, 0:E], ALU.mult))
            step(v.tensor_reduce(tab[:, j:j + 1], inj[:], AX.X, ALU.add))
        step(v.tensor_scalar(tab[:, EXTRA_MAX:], ext2[:, E - 1:E], float(E), None, ALU.add))
        v.tensor_copy(table[:], tab[:]).then_inc(routed, 1)

        def select_tokens():
            for b in range(NBLK):
                ins = v.tensor_scalar(gat1[:, b, :], iota[:], pos[:, 0, b:b + 1], None, ALU.is_equal)
            return ins

        def select_second():
            for b in range(NBLK):
                ins = v.scalar_tensor_tensor(out=sel[:, b, :], in0=iota[:], scalar=pos[:, 1, b:b + 1],
                                             in1=gat1[:, b, :], op0=ALU.is_equal, op1=ALU.add)
            return ins

        step(select_tokens())
        select_second().then_inc(sel_ready, 1)

        def gather_lo(n):
            ve.wait_ge(gath, n)
            for q, bank in ((0, 7), (1, 0)):
                ins = v.tensor_copy(xs_lo[:, 4 * q:4 * q + 4, :], ps[:, bank, :].rearrange("p (b c) -> p b c", c=P))
            ins.then_inc(xlo, 1)

        gather_lo(1)
        step(v.memset(facc[:], 0.0))
        lo_to(S_MOE)
        ve.wait_ge(routed, 1)
        n_items = ve.value_load(table[0:1, EXTRA_MAX:EXTRA_MAX + 1], min_val=E, max_val=E + EXTRA_MAX)

        with ve.Fori(0, n_items) as i:
            def e_lo_unit(j, s=None):
                lo_loop(U_MOE, S_MOE, j, i * N_FFN if s is None else i * N_FFN + s * 6)

            def e_mul(s):
                if s is None:
                    ve.wait_ge(split_used, i * N_FFN + (S_MOE + 4))
                    ve.wait_ge(e_si, i * NSTEP + 1)
                else:
                    ve.wait_ge(split_used, i * N_FFN + s * 6 + (S_MOE - 2 + 4))
                    ve.wait_ge(e_si, i * NSTEP + s + 1)
                v.tensor_tensor(e_g[:], e_silu[:], ps[:, 1, :], ALU.mult).then_inc(e_mu, 1)

            def gt_split(n):
                ve.wait_ge(e_hi, n)
                v.tensor_tensor(gt_lo[:], ps[:, 2, :].rearrange("p (a b) -> p a b", b=P),
                                gt_hi[:].bitcast(F32), ALU.subtract).then_inc(e_lo, 1)

            G = 4
            for b in range(NBLK):
                ins = v.tensor_scalar(gat1[:, b, :], iota[:], pos[:, 0, b:b + 1], gate[:, 0, b:b + 1],
                                      ALU.is_equal, ALU.mult)
                ins = v.tensor_scalar(gat[:, b, :], iota[:], pos[:, 1, b:b + 1], gate[:, 1, b:b + 1],
                                      ALU.is_equal, ALU.mult)
            ins.then_inc(own, 1)
            ve.wait_ge(own, i * G + 1)
            v.tensor_tensor(gat[:], gat[:], gat1[:], ALU.add).then_inc(gat_step, 1)
            v.tensor_scalar(pos[:], pos[:], -float(P), None, ALU.add).then_inc(own, 1)
            ve.wait_ge(own, i * G + 2)
            ve.wait_ge(gat_step, i * 2 + 1)
            select_tokens().then_inc(own, 1)
            ve.wait_ge(own, i * G + 3)
            select_second().then_inc(sel_ready, 1)
            for j in range(4):
                e_lo_unit(j)
            e_mul(None)
            with ve.Fori(1, NSTEP) as s:
                for j in range(4):
                    e_lo_unit(j - 2, s)
                gt_split(i * NSTEP + s)
                for j in range(4, 6):
                    e_lo_unit(j - 2, s)
                e_mul(s)
            gather_lo(i + 2)
            gt_split(i * NSTEP + NSTEP)
            for j in range(2):
                e_lo_unit(4 + 6 * 6 + j)
            for k in range(KD):
                ve.wait_ge(scat, i * KD + k + 1)
                v.tensor_tensor(facc[:, k, :], facc[:, k, :], ps[:, 5 + k % 3, 0:T], ALU.add).then_inc(scat_add, 1)
            v.nop().then_inc(own, 1)
            v.nop().then_inc(gat_step, 1)
            ve.wait_ge(own, i * G + 4)
        nc.vector.nop().then_inc(own_end, 1)
        ve.wait_ge(own_end, 1)
        for k in range(0, KD, 2):
            residual(1, 5 * KD, k, facc[:, k:k + 2, :])

        ve.wait_ge(std_ready, 9)
        step(v.reciprocal(rstd[:], stdt[:]))
        for k in range(KD):
            v.scalar_tensor_tensor(out=hf[:, k, :], in0=x[:, k, :], scalar=vec[:, 0, R_FG + k:R_FG + k + 1],
                                   in1=rstd[:], op0=ALU.mult, op1=ALU.mult).then_inc(fin_t, 1)

    @block.tensor
    def _(pe):
        t_ = nc.tensor

        def mm3(out, a_hi, a_lo, b_hi, b_lo, first_, last_):
            t_.matmul(out, a_hi, b_hi, start=first_, stop=False)
            t_.matmul(out, a_hi, b_lo, start=False, stop=False)
            return t_.matmul(out, a_lo, b_hi, start=False, stop=last_)

        pe.wait_ge(const, 1)
        pe.wait_ge(act_c, 1)
        for k in range(KD):
            ins = t_.transpose(ps[:, 0, k * ROWS:(k + 1) * ROWS], cs_row[:, k * P:(k + 1) * P], ident[0:ROWS, 0:ROWS])
        ins.then_inc(prep_tr, 1)
        pe.wait_ge(vec_in, 16 * N_VEC)
        for l in range(DEPTH):
            ins = t_.transpose(ps[:, 1, l * NV:(l + 1) * NV], vrow[:, l, :], ident[0:NV, 0:NV])
        ins.then_inc(prep_tr, 1)
        pe.wait_ge(x_in, 16 * N_X)
        for k in range(KD):
            if k >= 2:
                pe.wait_ge(x_cp, k - 1)
            for b in range(NBLK):
                n = BLK[b]
                ins = t_.transpose(ps[:, 2 + k % 2, b * P:b * P + n], xtok[0:n, b, k * P:(k + 1) * P],
                                   ident[0:n, 0:n])
            ins.then_inc(prep_tr, 1)

        def ada(l, c):
            n = 12 * l + c
            if n >= 2:
                pe.wait_ge(row_out, n - 1)
            for r in range(2):
                u = U_ADA[l] + 2 * c + r
                pe.wait_ge(raw_in[u % RAW], 16 * (u // RAW + 1))
                for k in range(KB):
                    ins = t_.matmul(ps[0:ROWS, 6 + c % 2, :], cT[:, r * KB + k, :], raw[:, u % RAW, k, :],
                                    start=(r == 0 and k == 0), stop=(r == 1 and k == KB - 1))
                ins.then_inc(plain_used, 1)

        def ada_tr(l, c):
            n = 12 * l + c
            pe.wait_ge(row_out, n + 1)
            if n >= 1:
                pe.wait_ge(mod_add, n)
            for m in range(4):
                ins = t_.transpose(ps[:, 5, m * ROWS:(m + 1) * ROWS],
                                   modrow[:, m * P:(m + 1) * P], ident[0:ROWS, 0:ROWS])
            ins.then_inc(row_tr, 1)

        pe.wait_ge(prep_cp, 1)
        ada(0, 0)
        ada(0, 1)
        pe.wait_ge(aux_in, 16 * (2 * NSEQ + 1))
        pe.wait_ge(gw_in, 16)
        for l in range(DEPTH):
            if l:
                pe.wait_ge(prep_cp, 3)
            for h in range(H):
                t_.transpose(ps[:, 4, h * P:(h + 1) * P], gw_raw[:, l * H + h, :], ident[:])
                ins = t_.transpose(ps[:, 5, h * NS_TOK:(h + 1) * NS_TOK], gs_raw[0:NS_TOK, l * H + h, :],
                                   ident[0:NS_TOK, 0:NS_TOK])
            ins.then_inc(prep_tr, 1)

        def buffers(l, bank):
            for gi in range(H):
                n = NSEQ * BUF
                ins = t_.transpose(ps[:, bank, gi * n:(gi + 1) * n], buf_raw[0:NSEQ * BUF, l, gi * P:(gi + 1) * P],
                                   ident[0:n, 0:n])
            ins.then_inc(prep_tr, 1)

        pe.wait_ge(prep_cp, 4)
        buffers(0, 4)
        pe.wait_ge(prep_cp, 5)
        buffers(1, 4)
        pe.wait_ge(prep_cp, 6)
        ada_tr(0, 0)
        for c in range(2, 12):
            ada(0, c)
            ada_tr(0, c - 1)
        ada_tr(0, 11)

        def sum_squares(n_sq, k0, k1, bank):
            for k in range(k0, k1):
                if k % 2 == 0:
                    pe.wait_ge(sq_ready, n_sq + (k - k0) // 2 + 1)
                ins = t_.matmul(ps[:, bank, 0:T], ones[:], sq[:, k, :], start=(k == k0), stop=(k == k1 - 1))
            ins.then_inc(ssum, 1)

        def unit(s):
            pe.wait_ge(lo_ready, s + 1)
            return w_hi[:, s % SPL], w_lo[:, s % SPL]

        def project_in(l):
            s = S_IN[l]
            for c in range(3):
                if c == 2:
                    pe.wait_ge(u_out, l + 1)
                for r in range(2):
                    wh, wl = unit(s + 2 * c + r)
                    for k in range(KB):
                        kk = r * KB + k
                        if c == 0:
                            pe.wait_ge(h_ready, 12 * l + kk // 2 + 1)
                        if c == 1:
                            for b in range(NBLK):
                                tk = slice(VBLK[b], VBLK[b] + P)
                                ins = mm3(ps[:, 4 + b, :], h_hi[:, kk, tk], h_lo[:, kk, tk], wh[:, k, :], wl[:, k, :],
                                          kk == 0, kk == KD - 1)
                        else:
                            for m in range(4):
                                mc = slice(m * P, (m + 1) * P)
                                out = ps[:, m, 0:T]
                                t_.matmul(out, wh[:, k, mc], h_hi[:, kk, 0:T], start=(kk == 0), stop=False)
                                t_.matmul(out, wh[:, k, mc], h_lo[:, kk, 0:T], start=False, stop=False)
                                ins = t_.matmul(out, wl[:, k, mc], h_hi[:, kk, 0:T], start=False, stop=(kk == KD - 1))
                    ins.then_inc(split_used, 1)

        def state_rows(l):
            pe.wait_ge(p_out, 2 * (l + 1))
            pe.wait_ge(v_out, l + 1)
            for gi in range(H):
                t_.transpose(ps[0:BUF, 3, gi * P:(gi + 1) * P], pp[:, gi, PADP + NP_TOK - BUF:], ident[:])
            for gi in range(H):
                ins = t_.transpose(ps[0:NS_TOK, 4, gi * P:(gi + 1) * P], sps[:, gi, :], ident[:])
            ins.then_inc(st_tr, 1)

        def mix_gate(l):
            pe.wait_ge(masked, 1)
            pe.wait_ge(v_done, l + 1)
            pe.wait_ge(layer_in, 64 * (l + 1))
            pe.wait_ge(st_cp, l + 1)
            for h in range(H):
                hc = slice(h * P, (h + 1) * P)
                for n in range(2):
                    tk = slice(n * P, (n + 1) * P)
                    t_.matmul(ps[:, h, tk], v_norm[:, n, hc], gw[:, l, h, :], start=True, stop=False)
                    t_.matmul(ps[:, h, tk], ones[BIAS_ROW:BIAS_ROW + 1, :], g_bias[:, h, :], start=False, stop=True)
                tk = slice(NP_TOK, T)
                t_.matmul(ps[:, h, tk], v_norm[NS_TOK:P, 2, hc], gs[NS_TOK:P, l, h, :], start=True, stop=False)
                ins = t_.matmul(ps[:, h, tk], ones[BIAS_ROW:BIAS_ROW + 1, :],
                                g_bias[:, h, 0:TS].unsqueeze(1).to_broadcast([1, NSEQ, TS]),
                                start=False, stop=True)
            ins.then_inc(gate_mm, 1)

        def mix_pool(l):
            pe.wait_ge(d_done, l + 1)
            pe.wait_ge(layer_in, 64 * (l + 1))
            pe.wait_ge(st_cp, l + 1)
            for gi in range(H):
                if gi:
                    pe.wait_ge(yb_done, H * l + gi)
                dj, djs = (wb, wsb) if gi % 2 == 0 else (wa, wsa)
                t_.matmul(ps[:, 4, 0:NP_TOK], pw[:, gi, :], dj[:, gi, PADP:], start=True, stop=True)
                t_.matmul(ps[:, 4, NP_TOK:T], pw[:, gi, :], djs[:, gi, :, BUF:], start=True,
                          stop=True).then_inc(pool_mm, 1)

        def project_out(l):
            s = S_OUT[l]
            for c in range(2):
                for r in range(2):
                    wh, wl = unit(s + 2 * c + r)
                    pe.wait_ge(h_ready, 12 * l + 4 + 4)
                    for k in range(KB):
                        kk = r * KB + k
                        for m in range(4):
                            mc = slice(m * P, (m + 1) * P)
                            out = ps[:, 4 * c + m, 0:T]
                            t_.matmul(out, wh[:, k, mc], h_hi[:, kk, 0:T], start=(kk == 0), stop=False)
                            t_.matmul(out, wh[:, k, mc], h_lo[:, kk, 0:T], start=False, stop=False)
                            ins = t_.matmul(out, wl[:, k, mc], h_hi[:, kk, 0:T], start=False, stop=(kk == KD - 1))
                    ins.then_inc(split_used, 1)

        sum_squares(0, 0, KD, 0)
        project_in(0)
        pe.wait_ge(v_out, 1)
        ada(1, 0)
        state_rows(0)
        ada(1, 1)
        ada_tr(1, 0)
        ada(1, 2)
        ada_tr(1, 1)
        mix_pool(0)
        sum_squares(4, H, KD, 4)
        ada(1, 3)
        ada_tr(1, 2)
        mix_gate(0)
        ada(1, 4)
        ada_tr(1, 3)
        ada(1, 5)
        ada_tr(1, 4)
        pe.wait_ge(ya_done, 1)
        sum_squares(6, 0, H, 0)
        for c in range(6, 12):
            ada(1, c)
            ada_tr(1, c - 1)
        ada_tr(1, 11)
        pe.wait_ge(mod_add, 24)
        project_out(0)
        sum_squares(8, 0, KD, 0)

        def up(base, u, s, wh, wl, r, bank0):
            for k in range(KB):
                kk = r * KB + k
                for m in range(4):
                    mc = slice(m * P, (m + 1) * P)
                    out = ps[:, bank0 + m, 0:T]
                    t_.matmul(out, wh[:, k, mc], h_hi[:, kk, 0:T], start=(kk == 0), stop=False)
                    t_.matmul(out, wh[:, k, mc], h_lo[:, kk, 0:T], start=False, stop=False)
                    ins = t_.matmul(out, wl[:, k, mc], h_hi[:, kk, 0:T], start=False, stop=(kk == KD - 1))
            ins.then_inc(split_used, 1)

        def down(wh, wl, bank0):
            for k in range(KB):
                for m in range(4):
                    mc = slice(m * P, (m + 1) * P)
                    out = ps[:, bank0 + m, 0:T]
                    t_.matmul(out, wh[:, k, mc], g_hi[:, k, :], start=(k == 0), stop=False)
                    t_.matmul(out, wh[:, k, mc], g_lo[:, k, :], start=False, stop=False)
                    ins = t_.matmul(out, wl[:, k, mc], g_hi[:, k, :], start=False, stop=(k == KB - 1))
            ins.then_inc(split_used, 1)

        def ffn_unit(j, per):
            pe.wait_ge(lo_ready, per + (S_FFN + 4 + j + 1))
            sl = (S_FFN + 4 + j) % SPL
            return w_hi[:, sl], w_lo[:, sl]

        pe.wait_ge(h_ready, 12)
        for j in range(4):
            up(None, None, None, *unit(S_FFN + j), j % 2, 4 * (j // 2))

        def ffn_down(s):
            pe.wait_ge(f_lo, s)

        with pe.Fori(1, NSTEP) as s:
            per = (s - 1) * 6
            for j in range(4):
                if j == 0:
                    pe.wait_ge(f_add, s * 2 - 1)
                    pe.wait_ge(f_silu, s)
                if j == 2:
                    pe.wait_ge(f_add, s * 2 - 1)
                    pe.wait_ge(f_mul, s)
                    pe.wait_ge(f_add, s * 2 - 1)
                up(None, None, None, *ffn_unit(j, per), j % 2, 4 * (j // 2))
            ffn_down(s)
            pe.wait_ge(f_silu, s + 1)
            down(*ffn_unit(4, per), 0)
            pe.wait_ge(f_mul, s + 1)
            down(*ffn_unit(5, per), 4)
        pe.wait_ge(f_add, 13)
        pe.wait_ge(f_lo, 7)
        down(*unit(S_FFN + 40), 0)
        down(*unit(S_FFN + 41), 4)

        sum_squares(12, 0, KD, 0)
        project_in(1)
        state_rows(1)
        mix_pool(1)
        sum_squares(16, H, KD, 4)
        mix_gate(1)
        pe.wait_ge(ya_done, 2)
        sum_squares(18, 0, H, 0)
        project_out(1)
        sum_squares(20, 0, KD, 0)

        pe.wait_ge(rw_in, 16)
        pe.wait_ge(scaled, 16)
        pe.wait_ge(affine, 32)
        for b in range(NBLK):
            n = BLK[b]
            for k in range(KD):
                ins = t_.matmul(ps[0:n, 0, b * E:(b + 1) * E], hf[:, k, b * P:b * P + n], rw[:, k, :],
                                start=(k == 0), stop=(k == KD - 1))
        ins.then_inc(log_mm, 1)
        for b in range(NBLK):
            n = BLK[b]
            for k in range(KD):
                ins = t_.transpose(ps[0:n, 2 + 2 * b + k // 4, (k % 4) * P:(k % 4 + 1) * P],
                                   hf[:, k, b * P:b * P + n], ident[:])
            ins.then_inc(tok_tr, 1)
        pe.wait_ge(chosen_r, 1)
        for b in range(NBLK):
            n = BLK[b]
            for q in range(b):
                t_.matmul(ps[0:n, 1, b * E:(b + 1) * E], ones[:, 0:n], chosen[:, q, :], start=(q == 0), stop=False)
            t_.matmul(ps[0:n, 1, b * E:(b + 1) * E], below[0:n, 0:n], chosen[0:n, b, :], start=(b == 0), stop=True)
        for b in range(NBLK):
            n = BLK[b]
            ins = t_.matmul(ps[:, 1, NBLK * E:(NBLK + 1) * E], ones[0:n, :], chosen[0:n, b, :], start=(b == 0),
                            stop=(b == NBLK - 1))
        ins.then_inc(rank_mm, 1)

        def gather():
            for src, banks in ((ht_hi, (5, 6)), (ht_lo, (7, 0))):
                for k in range(KD):
                    out = ps[:, banks[k // 4], (k % 4) * P:(k % 4 + 1) * P]
                    for b in range(NBLK):
                        n = BLK[b]
                        ins = t_.matmul(out, src[0:n, b, k * P:(k + 1) * P], sel[0:n, b, :], start=(b == 0),
                                        stop=(b == NBLK - 1))
            ins.then_inc(gath, 1)

        pe.wait_ge(tok_lo, NBLK)
        pe.wait_ge(sel_ready, 1)
        gather()
        pe.wait_ge(routed, 1)
        n_items = pe.value_load(table[0:1, EXTRA_MAX:EXTRA_MAX + 1], min_val=E, max_val=E + EXTRA_MAX)

        with pe.Fori(0, n_items) as i:
            def e_unit(j, s=None):
                k = i * N_FFN if s is None else i * N_FFN + s * 6
                pe.wait_ge(lo_ready, k + (S_MOE + j + 1))
                return w_hi[:, (S_MOE + j) % SPL], w_lo[:, (S_MOE + j) % SPL]

            def e_up(w, r, bank):
                for k in range(KB):
                    kk = r * KB + k
                    ins = mm3(ps[:, bank, :], xs_hi[:, kk, :], xs_lo[:, kk, :], w[0][:, k, :], w[1][:, k, :],
                              kk == 0, kk == KD - 1)
                ins.then_inc(split_used, 1)

            def e_transpose(n):
                pe.wait_ge(e_mu, n)
                for m in range(KB):
                    ins = t_.transpose(ps[:, 2, m * P:(m + 1) * P], e_g[:, m * P:(m + 1) * P], ident[:])
                ins.then_inc(e_tr, 1)

            def e_down(w, c, first_, last_):
                for k in range(KB):
                    ins = mm3(ps[:, 3 + c, :], gt_hi[:, k, :], gt_lo[:, k, :], w[0][:, k, :], w[1][:, k, :],
                              first_ and k == 0, last_ and k == KB - 1)
                ins.then_inc(split_used, 1)

            def e_step(s, j0, sreg, first_):
                pe.wait_ge(e_si, i * NSTEP + s)
                e_up(e_unit(j0, sreg), 0, 0)
                e_up(e_unit(j0 + 1, sreg), 1, 0)
                e_transpose(i * NSTEP + s)
                e_up(e_unit(j0 + 2, sreg), 0, 1)
                e_up(e_unit(j0 + 3, sreg), 1, 1)
                pe.wait_ge(e_lo, i * NSTEP + s)
                for c in range(2):
                    e_down(e_unit(j0 + 4 + c, sreg), c, first_, False)

            pe.wait_ge(xhi, i + 1)
            pe.wait_ge(xlo, i + 1)
            for j in range(4):
                e_up(e_unit(j), j % 2, j // 2)
            e_step(1, 4, None, True)
            with pe.Fori(2, NSTEP) as s:
                e_step(s, -2, s, False)
            pe.wait_ge(sel_ready, i + 2)
            pe.wait_ge(e_si, i * NSTEP + NSTEP)
            gather()
            e_transpose(i * NSTEP + NSTEP)
            pe.wait_ge(gat_step, i * 2 + 1)
            for b in range(NBLK):
                n = BLK[b]
                ins = t_.transpose(ps[:, 1, b * P:b * P + n], gat[0:n, b, :], ident[0:n, 0:n])
            ins.then_inc(gat_tr, 1)
            pe.wait_ge(e_lo, i * NSTEP + NSTEP)
            for c in range(2):
                e_down(e_unit(40 + c), c, False, True)
            pe.wait_ge(y_cp, i + 1)
            pe.wait_ge(gat_cp, i + 1)
            pe.wait_ge(xhi, i + 2)
            pe.wait_ge(xlo, i + 2)
            for k in range(KD):
                if k >= 3:
                    pe.wait_ge(scat_add, i * KD + k - 2)
                t_.matmul(ps[:, 5 + k % 3, 0:T], e_y[:, k * P:(k + 1) * P], gatT[:], start=True,
                          stop=True).then_inc(scat, 1)

        pe.wait_ge(own_end, 1)
        sum_squares(24, 0, KD, 0)
        pe.wait_ge(fin_t, KD)
        for b in range(NBLK):
            n = BLK[b]
            for k in range(KD):
                ins = t_.transpose(ps[0:n, 2 + 2 * b + k // 4, (k % 4) * P:(k % 4 + 1) * P],
                                   hf[:, k, b * P:b * P + n], ident[:])
            ins.then_inc(fin_tr, 1)


def kernel(**inputs):
    import concourse.bacc as bacc
    from concourse.bass_utils import run_bass_kernel_spmd
    nc = bacc.Bacc("TRN2", target_bir_lowering=False, num_devices=1, dynamic_dma_scratch_size=1024)
    build_program(nc)
    arrays = {f"in_{n}": np.ascontiguousarray(a) for n, a in inputs.items()}
    r = run_bass_kernel_spmd(nc, [arrays], core_ids=[0]).results[0]
    return tuple(r[f"out_{i}"] for i in range(6))
```

```python
from contextlib import ExitStack

import numpy as np

import concourse.bass as bass
import concourse.mybir as mybir

F32 = mybir.dt.float32
F32R = mybir.dt.float32r
I32 = mybir.dt.int32
U32 = mybir.dt.uint32
ALU = mybir.AluOpType
ACT = mybir.ActivationFunctionType
AX = mybir.AxisListType

P = 128
D = 1024
KD = D // P
DEPTH = 2
NP_TOK = 256
NSEQ = 8
TS = 8
NS_TOK = NSEQ * TS
T = NP_TOK + NS_TOK
VBLK = (0, P, T - P)
BLK = [P, P, NS_TOK]
NBLK = len(BLK)
ROWS = 1 + NSEQ
NMOD = 6 * KD
H = 4
HALF = 512
BUF = 15
WIN = (2, 4, 8, 16)
BIAS_ROW = 96
PADP = 16
DFF = 3584
B = 512
KB = B // P
NSTEP = DFF // B
E = 8
EPS = 1e-6
NV = 84
R_N1, R_N2, R_ADAB, R_PS, R_AG, R_BG, R_FG = 0, 8, 16, 64, 68, 72, 76

RAW = 6
SPL = 3
EXTRA_MAX = 4

N_IN, N_OUT, N_FFN = 6, 4, 6 * NSTEP
FIRST_MOD = [(0, c) for c in range(4)]
MIXER_MOD = ([(0, c) for c in range(4, 12)], [(1, c) for c in range(6, 12)])
NORM_MOD = {1: [(1, c) for c in range(4)], 2: [(1, 4), (1, 5)]}
PARTS = [("ada", FIRST_MOD), ("in", 0), ("ada", MIXER_MOD[0]), ("out", 0), ("ada", NORM_MOD[1]), ("ffn", 0),
         ("ada", NORM_MOD[2]), ("in", 1), ("ada", MIXER_MOD[1]), ("out", 1)]
KIND = []
BLOCK = {}
START, START_S = {}, {}
n_plain = n_split = 0
for part, what in PARTS:
    if part == "ada":
        for key in what:
            BLOCK[key] = n_plain // 2
            KIND += [(True, n_plain), (True, n_plain + 1)]
            n_plain += 2
    else:
        START[part, what], START_S[part, what] = len(KIND), n_split
        for _ in range({"in": N_IN, "out": N_OUT, "ffn": N_FFN}[part]):
            KIND.append((False, n_split))
            n_split += 1
U_OF_PLAIN = [u for u, (plain, _) in enumerate(KIND) if plain]
U_OF_SPLIT = [u for u, (plain, _) in enumerate(KIND) if not plain]
U_MOE, S_MOE = len(KIND), n_split
S_IN = [START_S["in", l] for l in range(DEPTH)]
S_OUT = [START_S["out", l] for l in range(DEPTH)]
U_FFN, S_FFN = START["ffn", 0], START_S["ffn", 0]


def build_program(nc):
    shapes = {
        'x_prompt': (1, NP_TOK, D), 'x_sample': (NSEQ, TS, D), 'state_pool': (DEPTH, NSEQ, BUF, HALF),
        'c_prompt': (1, D), 'c_sample': (NSEQ, D), 'norm1_g': (DEPTH, D), 'norm2_g': (DEPTH, D),
        'ada_w': (DEPTH, D, 6 * D), 'ada_b': (DEPTH, 6 * D), 'w_in': (DEPTH, D, 3 * HALF),
        'v_norm_g': (DEPTH, HALF), 'v_norm_b': (DEPTH, HALF), 'sgu_w': (DEPTH, H, P, P), 'sgu_b': (DEPTH, H, P),
        'pool_w': (DEPTH, H, P, P), 'pool_scale': (DEPTH, HALF), 'branch_a_g': (DEPTH, HALF),
        'branch_b_g': (DEPTH, HALF), 'w_out': (DEPTH, D, D), 'ffn_w1': (1, D, DFF), 'ffn_w3': (1, D, DFF),
        'ffn_w2': (1, DFF, D), 'router_w': (1, D, E), 'moe_w1': (1, E, D, DFF), 'moe_w3': (1, E, D, DFF),
        'moe_w2': (1, E, DFF, D), 'final_g': (D,),
    }
    out_shapes = [(1, NP_TOK, D), (NSEQ, TS, D), (DEPTH, 1, BUF, HALF), (DEPTH, NSEQ, BUF, HALF),
                  (DEPTH, 1, P, HALF), (DEPTH, NSEQ, TS, HALF)]
    d = {n: nc.dram_tensor(f"in_{n}", s, F32, kind="ExternalInput").ap() for n, s in shapes.items()}
    o = [nc.dram_tensor(f"out_{i}", s, F32, kind="ExternalOutput").ap() for i, s in enumerate(out_shapes)]
    with ExitStack() as ctx:
        write_program(nc, ctx, d, o)


def write_program(nc, ctx, d, o):
    def sb(name, shape, dt=F32):
        return ctx.enter_context(nc.sbuf_tensor(name, shape, dt))

    def sem(name):
        return ctx.enter_context(nc.semaphore(name))

    raw = sb("raw", [P, RAW, KB, B])
    w_hi = sb("w_hi", [P, SPL, KB, B], F32R)
    w_lo = sb("w_lo", [P, SPL, KB, B], F32R)
    x = sb("x", [P, KD, T])
    hf = sb("hf", [P, KD, T])
    sq = hf
    rstd = sb("rstd", [P, T])
    stdt = rstd
    mod = sb("mod", [P, DEPTH, NMOD, ROWS])
    gain = sb("gain", [P, DEPTH, 2, KD, ROWS])
    modrow = sb("modrow", [ROWS, B])
    cT = sb("cT", [P, KD, ROWS])
    vec = sb("vec", [P, DEPTH, NV])
    ident = sb("ident", [P, P])
    ones = sb("ones", [P, P])
    below = sb("below", [P, P])
    iota = sb("iota", [P, P])
    eps = sb("eps", [P, 1])
    vng = sb("vng", [P, HALF])
    vnb = sb("vnb", [P, HALF])
    pw = sb("pw", [P, H, P])
    gw = sb("gw", [P, DEPTH, H, P])
    gs = sb("gs", [P, DEPTH, H, NS_TOK])
    pp = sb("pp", [P, H, PADP + NP_TOK])
    sp_ = sb("sp_", [P, DEPTH, H, NSEQ, BUF + TS])
    rcnt = sb("rcnt", [P, H, PADP])
    first = sb("first", [P, H, PADP])
    pst = sb("pst", [P, HALF])
    g_bias = pst[BIAS_ROW:BIAS_ROW + 1].rearrange("p (h t) -> p h t", t=P)
    v_stat = sb("v_stat", [P, NBLK * H, 6])
    v_mv = sb("v_mv", [P, NBLK * H, 2])
    v_std = sb("v_std", [P, NBLK * H])
    v_rstd = sb("v_rstd", [P, NBLK * H])
    smp = sb("smp", [P, 2, NS_TOK])
    rw = sb("rw", [P, KD, E])
    logit = sb("logit", [P, NBLK, E])
    top = sb("top", [P, NBLK, 8])
    topi = sb("topi", [P, NBLK, 8], U32)
    topf = sb("topf", [P, NBLK, 8])
    oh = sb("oh", [P, 2, NBLK, E])
    chosen = sb("chosen", [P, NBLK, E])
    rank = sb("rank", [P, NBLK, E])
    over1 = sb("over1", [P, NBLK, E])
    posn = sb("posn", [P, NBLK, E])
    tmpe = sb("tmpe", [P, NBLK, E])
    pos = sb("pos", [P, 2, NBLK])
    gate = sb("gate", [P, 2, NBLK])
    dtop = sb("dtop", [P, NBLK])
    etop = sb("etop", [P, NBLK])
    dsum = sb("dsum", [P, NBLK])
    cnt = sb("cnt", [P, E])
    ext = sb("ext", [P, E])
    ext2 = sb("ext2", [P, E])
    ebase = sb("ebase", [P, E])
    eoff = sb("eoff", [P, E])
    tab = sb("tab", [P, EXTRA_MAX + 1])
    inj = sb("inj", [P, E])
    inj2 = sb("inj2", [P, E])
    table = sb("table", [P, EXTRA_MAX + 1], I32)

    def views(name, dt, *phases):
        size = max(sum(int(np.prod(sh)) for sh in ph) for ph in phases)
        area = sb(name, [P, size], dt)
        out = []
        for ph in phases:
            at, got = 0, []
            for sh in ph:
                n = int(np.prod(sh))
                v = area[:, at:at + n]
                if len(sh) == 2:
                    v = v.rearrange("p (a b) -> p a b", b=sh[1])
                elif len(sh) == 3:
                    v = v.rearrange("p (a b c) -> p a b c", b=sh[1], c=sh[2])
                got.append(v)
                at += n
            out.append(got)
        return out

    (h_hi, h_lo, g_hi, g_lo), (ht_hi, ht_lo, xs_hi, xs_lo, gt_hi, gt_lo, sel) = views(
        "split", F32R,
        [(KD, T), (KD, T), (KB, T), (KB, T)],
        [(NBLK, D), (NBLK, D), (KD, P), (KD, P), (KB, P), (KB, P), (NBLK, P)])
    ((_, xtok, gw_raw, gs_raw, buf_raw), (uT, v_gelu, v_norm, wa, wb, wsa, wsb), (facc, _, silu_t),
     (_, _, e_silu, e_g, e_y, gat, gat1, gatT)) = views(
        "plain", F32,
        [(H, T), (NBLK, D), (DEPTH * H, P), (DEPTH * H, P), (DEPTH, HALF)],
        [(H, T), (NBLK, HALF), (NBLK, HALF), (H, PADP + NP_TOK), (H, PADP + NP_TOK),
         (H, NSEQ, BUF + TS), (H, NSEQ, BUF + TS)],
        [(KD, T), (H * T + NBLK * D - KD * T,), (KB, T)],
        [(KD, T), (H * T + NBLK * D - KD * T,), (B,), (B,), (D,), (NBLK, P), (NBLK, P), (T,)])
    g_f = silu_t
    yb = v_gelu.rearrange("p a b -> p (a b)")[:, 0:H * T].rearrange("p (a b) -> p a b", b=T)
    hrow = hf[:].rearrange("p a b -> p (a b)")
    crow, cs_row = hrow[0:ROWS, 0:D], hrow[0:ROWS, D:2 * D]
    vrow = hrow[0:NV, 2 * D:2 * D + DEPTH * P].rearrange("p (a b) -> p a b", b=P)
    NEWROWS = NS_TOK + BUF
    sps = hrow[:, 0:H * NEWROWS].rearrange("p (h t) -> p h t", t=NEWROWS)
    iota_i = rstd[:, 0:P].bitcast(I32)

    ps = ctx.enter_context(nc.psum_tensor("ps", [P, 8, 512], F32))

    raw_in = [sem(f"raw_in{i}") for i in range(RAW)]
    hi_ready = sem("hi_ready")
    lo_ready = sem("lo_ready")
    split_used = sem("split_used")
    plain_used = sem("plain_used")
    c_in = sem("c_in")
    vec_in = sem("vec_in")
    x_in = sem("x_in")
    aux_in = sem("aux_in")
    gw_in = sem("gw_in")
    rw_in = sem("rw_in")
    y_stored = sem("y_stored")
    zeroed = sem("zeroed")
    const = sem("const")
    pool_step = sem("pool_step")
    dve = sem("dve")
    act_c = sem("act_c")
    prep_tr = sem("prep_tr")
    prep_cp = sem("prep_cp")
    masked = sem("masked")
    row_out = sem("row_out")
    row_tr = sem("row_tr")
    mod_add = sem("mod_add")
    mod_ready = sem("mod_ready")
    x_cp = sem("x_cp")
    x_new = sem("x_new")
    sq_ready = sem("sq_ready")
    ssum = sem("ssum")
    std_ready = sem("std_ready")
    scaled = sem("scaled")
    affine = sem("affine")
    hhi = sem("hhi")
    h_ready = sem("h_ready")
    u_out = sem("u_out")
    v_out = sem("v_out")
    p_out = sem("p_out")
    v_var = sem("v_var")
    v_sd = sem("v_sd")
    v_done = sem("v_done")
    win_s = sem("win_s")
    d_done = sem("d_done")
    gate_mm = sem("gate_mm")
    ya_done = sem("ya_done")
    pool_mm = sem("pool_mm")
    yb_done = sem("yb_done")
    st_tr = sem("st_tr")
    st_cp = sem("st_cp")
    stored = sem("stored")
    v_stored = sem("v_stored")
    f_silu = sem("f_silu")
    f_mul = sem("f_mul")
    f_hi = sem("f_hi")
    f_lo = sem("f_lo")
    f_add = sem("f_add")
    log_mm = sem("log_mm")
    tok_tr = sem("tok_tr")
    tok_hi = sem("tok_hi")
    tok_lo = sem("tok_lo")
    top_done = sem("top_done")
    exp_done = sem("exp_done")
    chosen_r = sem("chosen_r")
    rank_mm = sem("rank_mm")
    routed = sem("routed")
    sel_ready = sem("sel_ready")
    gat_step = sem("gat_step")
    gath = sem("gath")
    xhi = sem("xhi")
    xlo = sem("xlo")
    e_si = sem("e_si")
    e_mu = sem("e_mu")
    e_tr = sem("e_tr")
    e_hi = sem("e_hi")
    e_lo = sem("e_lo")
    gat_tr = sem("gat_tr")
    gat_cp = sem("gat_cp")
    y_cp = sem("y_cp")
    scat = sem("scat")
    scat_add = sem("scat_add")
    fin_t = sem("fin_t")
    mixed = sem("mixed")
    mixed_hi = sem("mixed_hi")
    layer_in = sem("layer_in")
    own = sem("own")
    y_end = sem("y_end")
    scat_end = sem("scat_end")
    add_end = sem("add_end")
    fin_tr = sem("fin_tr")
    fin_cp = sem("fin_cp")

    N_C, N_VEC, N_X, N_AUX = 2, 8, 3, 0

    block = ctx.enter_context(nc.Block())

    def wblock(w, r, c):
        return w[r * B:(r + 1) * B, c * B:(c + 1) * B].rearrange("(k p) n -> p k n", p=P)

    def step_units(w1, w3, w2, s):
        up = [wblock(w1, 0, s), wblock(w1, 1, s), wblock(w3, 0, s), wblock(w3, 1, s)] if s < NSTEP else []
        return up + ([wblock(w2, s - 1, 0), wblock(w2, s - 1, 1)] if s else [])

    def dyn_units(w1, w3, w2, s):
        def blk(w, r):
            return w[r * B:(r + 1) * B, bass.ts(s, B)].rearrange("(k p) n -> p k n", p=P)
        down = w2[bass.ts(s - 1, B), :]
        return [blk(w1, 0), blk(w1, 1), blk(w3, 0), blk(w3, 1)] + [
            down[:, c * B:(c + 1) * B].rearrange("(k p) n -> p k n", p=P) for c in range(2)]

    @block.sync
    def _(sp):
        def load(u, src):
            if u >= RAW:
                plain, n = KIND[u - RAW]
                sp.wait_ge(plain_used if plain else lo_ready, n + 1)
            sp.dma_start(raw[:, u % RAW], src).then_inc(raw_in[u % RAW], 16)

        def load_ada(blocks):
            for l, c in blocks:
                for r in range(2):
                    load(U_OF_PLAIN[2 * BLOCK[l, c] + r], wblock(d['ada_w'][l], r, c))

        def load_in(l):
            for c in range(3):
                for r in range(2):
                    load(U_OF_SPLIT[S_IN[l] + 2 * c + r], wblock(d['w_in'][l], r, c))

        def load_out(l):
            for c in range(2):
                for r in range(2):
                    load(U_OF_SPLIT[S_OUT[l] + 2 * c + r], wblock(d['w_out'][l], r, c))

        load_ada(FIRST_MOD)
        load_in(0)
        load_ada(MIXER_MOD[0])
        load_out(0)
        load_ada(NORM_MOD[1])
        w = (d['ffn_w1'][0], d['ffn_w3'][0], d['ffn_w2'][0])
        for j, src in enumerate(step_units(*w, 0)):
            load(U_FFN + j, src)
        sp.wait_ge(plain_used, 2 * BLOCK[NORM_MOD[1][-1]] + 2)
        with sp.Fori(1, NSTEP) as s:
            for j, src in enumerate(dyn_units(*w, s)):
                sp.wait_ge(lo_ready, s * 6 + (S_FFN + 4 - 6 + j - RAW + 1))
                slot = (U_FFN + 4 + j) % RAW
                sp.dma_start(raw[:, slot], src).then_inc(raw_in[slot], 16)
        for j, src in enumerate(step_units(*w, NSTEP)):
            load(U_FFN + 4 + 6 * (NSTEP - 1) + j, src)
        load_ada(NORM_MOD[2])
        load_in(1)
        load_ada(MIXER_MOD[1])
        load_out(1)

        def load_item(i, e):
            w = (d['moe_w1'][0, e], d['moe_w3'][0, e], d['moe_w2'][0, e])

            def put(j, src, s=None):
                n = i * N_FFN + (S_MOE + j - RAW + 1)
                sp.wait_ge(lo_ready, n if s is None else n + s * 6)
                slot = (U_MOE + j) % RAW
                sp.dma_start(raw[:, slot], src).then_inc(raw_in[slot], 16)

            for j, src in enumerate(step_units(*w, 0)):
                put(j, src)
            with sp.Fori(1, NSTEP) as s:
                for j, src in enumerate(dyn_units(*w, s)):
                    put(4 - 6 + j, src, s)
            for j, src in enumerate(step_units(*w, NSTEP)):
                put(4 + 6 * (NSTEP - 1) + j, src)

        sp.wait_ge(plain_used, 2 * BLOCK[MIXER_MOD[1][-1]] + 2)
        with sp.Fori(0, E) as e:
            load_item(e, e)
        sp.wait_ge(routed, 1)
        n_items = sp.value_load(table[0:1, EXTRA_MAX:EXTRA_MAX + 1], min_val=E, max_val=E + EXTRA_MAX)
        with sp.If(n_items > E):
            with sp.Fori(E, n_items) as i:
                ex = sp.value_load(table[0:1, bass.ds(i - E, 1)], min_val=0, max_val=E - 1)
                load_item(i, ex)
            sp.nop()
        for b in range(NBLK):
            n = BLK[b]
            sp.wait_ge(fin_cp, b + 1)
            dst = o[0][0, b * P:(b + 1) * P, :] if b < 2 else o[1].rearrange("b t d -> (b t) d")
            sp.dma_start(dst, xtok[0:n, b, :]).then_inc(y_stored, 16)
        sp.wait_ge(y_stored, 16 * NBLK)
        sp.wait_ge(stored, 16 * DEPTH * 3)
        sp.wait_ge(v_stored, 16 * DEPTH * 2)

    @block.gpsimd
    def _(gp):
        steps = [0]

        def step(ins):
            steps[0] += 1
            ins.then_inc(pool_step, 1)
            gp.wait_ge(pool_step, steps[0])

        def load_layer(l):
            gp.dma_start(pw[:], d['pool_w'][l].rearrange("g c e -> c g e")).then_inc(layer_in, 16)
            gp.dma_start(g_bias, d['sgu_b'][l:l + 1]).then_inc(layer_in, 16)
            gp.dma_start(vng[:], d['v_norm_g'][l].partition_broadcast(P)).then_inc(layer_in, 16)
            gp.dma_start(vnb[:], d['v_norm_b'][l].partition_broadcast(P)).then_inc(layer_in, 16)

        g = nc.gpsimd
        step(g.memset(ident[:], 0.0))
        step(g.affine_select(out=ident[:], in_=ident[:], compare_op=ALU.not_equal, fill=1.0, base=0,
                             pattern=[[-1, P]], channel_multiplier=1))
        step(g.memset(ones[:], 1.0))
        step(g.memset(gs_raw, 0.0))
        g.memset(eps[:], EPS).then_inc(const, 1)
        for b in range(NSEQ):
            for l in range(DEPTH):
                gp.dma_start(gs_raw[b * TS:(b + 1) * TS, l * H:(l + 1) * H, NS_TOK + b * TS:NS_TOK + (b + 1) * TS],
                             d['sgu_w'][l, :, 0:TS, 0:TS].rearrange("h t s -> t h s")).then_inc(aux_in, 16)
        gp.dma_start(buf_raw[0:NSEQ * BUF], d['state_pool'].rearrange("l b r c -> (b r) l c")).then_inc(aux_in, 16)
        load_layer(0)
        for l in range(DEPTH):
            gp.dma_start(o[3][l, :, 0:BUF - TS, :], d['state_pool'][l, :, TS:BUF, :]).then_inc(stored, 16)
        g.affine_select(out=below[:], in_=ones[:], compare_op=ALU.is_gt, fill=0.0, base=0,
                        pattern=[[1, P]], channel_multiplier=-1)
        step(g.iota(iota_i[:], pattern=[[1, P]], base=0, channel_multiplier=0))
        step(g.tensor_copy(iota[:], iota_i[:]))
        g.memset(pp[:, :, 0:PADP], 0.0)
        g.memset(logit[:], 0.0).then_inc(zeroed, 1)
        gp.wait_ge(prep_cp, 4)
        step(g.affine_select(out=gw[:], in_=gw[:], compare_op=ALU.is_ge, fill=0.0, base=0,
                             pattern=[[0, DEPTH * H], [1, P]], channel_multiplier=-1))
        g.affine_select(out=gs[:], in_=gs[:], compare_op=ALU.is_ge, fill=0.0, base=P - NS_TOK,
                        pattern=[[0, DEPTH * H], [1, NS_TOK]], channel_multiplier=-1).then_inc(masked, 1)

        for l in range(DEPTH):
            gp.wait_ge(p_out, 2 * (l + 1))
            ssrc = sp_[:, l]
            for j, w in enumerate(WIN):
                sdst, half = (wsb if j % 2 else wsa), w // 2
                ins = g.tensor_tensor(sdst[:, j:, :, w - 1:], ssrc[:, j:, :, w - 1:],
                                      ssrc[:, j:, :, w - 1 - half:BUF + TS - half], ALU.add)
                if j < 3:
                    step(ins)
                ssrc = sdst
            ins.then_inc(win_s, 1)
            gp.wait_ge(v_done, l + 1)
            gp.dma_start(o[4][l, 0], v_norm[:, 1, :]).then_inc(v_stored, 16)
            gp.dma_start(o[5][l].rearrange("b t c -> (b t) c"), v_norm[NS_TOK:P, 2, :]).then_inc(v_stored, 16)
            gp.wait_ge(st_cp, l + 1)
            gp.dma_start(o[2][l, 0], pst[NS_TOK:NS_TOK + BUF]).then_inc(stored, 16)
            gp.dma_start(o[3][l, :, BUF - TS:, :], pst[0:NS_TOK]).then_inc(stored, 16)
            if l + 1 < DEPTH:
                gp.wait_ge(gate_mm, l + 1)
                gp.wait_ge(pool_mm, H * (l + 1))
                load_layer(l + 1)

    @block.scalar
    def _(act):
        a = nc.scalar
        cur = [0]

        def hi(s, n=None):
            u = U_OF_SPLIT[s]
            act.wait_ge(raw_in[u % RAW], 16 * (u // RAW + 1))
            if s >= SPL:
                act.wait_ge(split_used, s - SPL + 1)
            a.activation(w_hi[:, s % SPL], raw[:, u % RAW], ACT.Copy).then_inc(hi_ready, 1)

        def hi_loop(u0, s0, j, t, per):
            act.wait_ge(raw_in[(u0 + j) % RAW], t * 16 + 16 * ((u0 + j) // RAW + 1))
            act.wait_ge(split_used, per + (s0 + j - SPL + 1))
            a.activation(w_hi[:, (s0 + j) % SPL], raw[:, (u0 + j) % RAW], ACT.Copy).then_inc(hi_ready, 1)

        def hi_to(s):
            while cur[0] < s:
                hi(cur[0])
                cur[0] += 1

        act.dma_start(crow[0:1, :], d['c_prompt']).then_inc(c_in, 16)
        act.dma_start(crow[1:ROWS, :], d['c_sample']).then_inc(c_in, 16)
        for r, name in ((R_N1, 'norm1_g'), (R_N2, 'norm2_g'), (R_ADAB, 'ada_b'), (R_PS, 'pool_scale'),
                        (R_AG, 'branch_a_g'), (R_BG, 'branch_b_g')):
            n = d[name].shape[1] // P
            act.dma_start(vrow[r:r + n], d[name].rearrange("l (j p) -> j l p", p=P)).then_inc(vec_in, 16)
        for l in range(DEPTH):
            act.dma_start(vrow[R_FG:R_FG + KD, l, :], d['final_g'].rearrange("(j p) -> j p", p=P)).then_inc(vec_in, 16)
        for b in range(2):
            act.dma_start(xtok[:, b, :], d['x_prompt'][0, b * P:(b + 1) * P, :]).then_inc(x_in, 16)
        act.dma_start(xtok[0:NS_TOK, 2, :], d['x_sample'].rearrange("b t d -> (b t) d")).then_inc(x_in, 16)
        act.dma_start(gw_raw, d['sgu_w'].rearrange("l h t s -> t (l h) s")).then_inc(gw_in, 16)
        act.dma_start(rw[:], d['router_w'][0].rearrange("(k p) e -> p k e", p=P)).then_inc(rw_in, 16)
        act.wait_ge(c_in, 16 * N_C)
        a.activation(cs_row[:], crow[:], ACT.Silu).then_inc(act_c, 1)

        def ada(l, c):
            n = BLOCK[l, c]
            act.wait_ge(plain_used, 2 * n + 2)
            if n >= 1:
                act.wait_ge(row_tr, n)
            a.activation(modrow[:], ps[0:ROWS, 6 + n % 2, :], ACT.Copy).then_inc(row_out, 1)

        def square(n0, src, k0, k1, wait):
            for k in range(k0, k1, 2):
                wait(k)
                a.activation(sq[:, k:k + 2, :], src(k), ACT.Square).then_inc(sq_ready, 1)

        def std(n, bank, width):
            act.wait_ge(ssum, n + 1)
            a.activation(stdt[:], ps[:, bank, 0:T], ACT.Sqrt, scale=1.0 / width, bias=eps[:]).then_inc(std_ready, 1)

        def norm(l, which):
            n = 2 * l + which
            for k in range(0, KD, 2):
                if n:
                    act.wait_ge(x_new, 4 * (n - 1) + k // 2 + 1)
                else:
                    act.wait_ge(x_cp, k + 2)
                a.activation(sq[:, k:k + 2, :], x[:, k:k + 2, :], ACT.Square).then_inc(sq_ready, 1)
            std(4 * l + 3 * which, 0, D)
            for b in range(KD // 2 + 1):
                if b < KD // 2:
                    act.wait_ge(scaled, 4 * n + b + 1)
                    for k in (2 * b, 2 * b + 1):
                        a.activation(hf[:, k, 0:NP_TOK], hf[:, k, 0:NP_TOK], ACT.Identity,
                                     scale=gain[:, l, which, k, 0:1],
                                     bias=mod[:, l, 3 * KD * which + k, 0:1]).then_inc(affine, 1)
                if b >= 1 and n < 3:
                    act.wait_ge(affine, 8 * n + 2 * b)
                    a.activation(h_hi[:, 2 * b - 2:2 * b, 0:T], hf[:, 2 * b - 2:2 * b, :], ACT.Copy).then_inc(hhi, 1)

        def project_in(l):
            s = S_IN[l]
            hi_to(s + 3)
            act.wait_ge(split_used, s + 2)
            if l:
                act.wait_ge(h_ready, 12 * l)
            a.activation(uT[:], ps[:, 0:H, 0:T], ACT.Gelu_apprx_tanh).then_inc(u_out, 1)
            hi_to(s + 5)
            act.wait_ge(split_used, s + 4)
            a.activation(v_gelu[:], ps[:, 4:4 + NBLK, :], ACT.Gelu_apprx_tanh).then_inc(v_out, 1)
            hi_to(s + 6)
            act.wait_ge(v_var, l + 1)
            a.activation(v_std[:], v_mv[:, :, 1], ACT.Sqrt, bias=eps[:]).then_inc(v_sd, 1)
            act.wait_ge(split_used, s + 6)
            a.activation(pp[:, :, PADP:], ps[:, 0:H, 0:NP_TOK], ACT.Copy).then_inc(p_out, 1)
            for gi in range(H):
                a.activation(sp_[:, l, gi, :, BUF:], ps[:, gi, NP_TOK:T].rearrange("p (b t) -> p b t", t=TS),
                             ACT.Copy)
            a.activation(sps[:, :, 0:NS_TOK], ps[:, 0:H, NP_TOK:T], ACT.Copy)
            a.activation(sps[:, :, NS_TOK:], ps[:, 0:H, NP_TOK - BUF:NP_TOK], ACT.Copy).then_inc(p_out, 1)
            act.wait_ge(st_tr, l + 1)
            if l:
                act.wait_ge(stored, 16 * (2 + 2 * l))
            a.activation(pst[0:NEWROWS], ps[0:NEWROWS, 4, :], ACT.Copy).then_inc(st_cp, 1)

        def mix_hi(l, k0, n_mix):
            for k in range(0, H, 2):
                act.wait_ge(mixed, n_mix + k // 2 + 1)
                a.activation(h_hi[:, k0 + k:k0 + k + 2, 0:T], hf[:, k0 + k:k0 + k + 2, :], ACT.Copy).then_inc(mixed_hi, 1)

        def mixer(l):
            f = MIXER_MOD[l]
            act.wait_ge(ya_done, l + 1)
            for k in range(0, H, 2):
                a.activation(sq[:, k:k + 2, :], uT[:, k:k + 2, :], ACT.Square).then_inc(sq_ready, 1)
            ada(*f[0])
            std(4 * l + 1, 0, HALF)
            mix_hi(l, 0, 4 * l)
            ada(*f[1])
            ada(*f[2])
            act.wait_ge(v_done, l + 1)
            for gi in range(H):
                act.wait_ge(pool_mm, H * l + gi + 1)
                a.activation(yb[:, gi, :], ps[:, 4, 0:T], ACT.Copy,
                             scale=vec[:, l, R_PS + gi:R_PS + gi + 1]).then_inc(yb_done, 1)
            for k in range(0, H, 2):
                act.wait_ge(yb_done, H * l + k + 2)
                a.activation(sq[:, H + k:H + k + 2, :], yb[:, k:k + 2, :], ACT.Square).then_inc(sq_ready, 1)
            ada(*f[3])
            std(4 * l + 2, 4, HALF)
            mix_hi(l, H, 4 * l + 2)
            for key in f[4:]:
                ada(*key)
            hi_to(S_OUT[l] + N_OUT)

        for key in FIRST_MOD:
            ada(*key)
        norm(0, 0)
        project_in(0)
        mixer(0)
        norm(0, 1)
        for key in NORM_MOD[1]:
            ada(*key)

        def ffn_silu(n):
            act.wait_ge(split_used, n[0])
            a.activation(silu_t[:], ps[:, 0:KB, 0:T], ACT.Silu).then_inc(f_silu, 1)

        def ffn_hi(used, mul):
            act.wait_ge(split_used, used)
            act.wait_ge(f_mul, mul)
            a.activation(g_hi[:], g_f[:], ACT.Copy).then_inc(f_hi, 1)

        s0 = S_FFN
        hi_to(s0 + 4)
        ffn_silu([s0 + 2])
        hi_to(s0 + 6)
        ffn_hi(s0 + 4, 1)
        u1, s1 = U_FFN + 4, S_FFN + 4
        with act.Fori(1, NSTEP - 1) as s:
            t = s - 1
            hi_loop(u1, s1, 2, t, t * 6)
            hi_loop(u1, s1, 3, t, t * 6)
            act.wait_ge(f_lo, s)
            ffn_silu([t * 6 + (s1 + 2)])
            for j in range(4, 8):
                hi_loop(u1, s1, j, t, t * 6)
            ffn_hi(t * 6 + (s1 + 6), s + 1)
        cur[0] = s1 + 6 * 5 + 2
        hi_to(cur[0] + 2)
        act.wait_ge(f_lo, 6)
        ffn_silu([s1 + 32])
        hi_to(cur[0] + 2)
        hi_to(cur[0] + 2)
        ffn_hi(s1 + 36, 7)
        norm(1, 0)
        for key in NORM_MOD[2]:
            ada(*key)
        project_in(1)
        mixer(1)
        norm(1, 1)

        for b in range(NBLK):
            n = BLK[b]
            act.wait_ge(tok_tr, b + 1)
            a.activation(ht_hi[0:n, b, :], ps[0:n, 2 + 2 * b:4 + 2 * b, :].rearrange("p a c -> p (a c)"),
                         ACT.Copy).then_inc(tok_hi, 1)
        act.wait_ge(top_done, 1)
        a.activation(etop[:], dtop[:], ACT.Exp).then_inc(exp_done, 1)

        def gather_hi(n):
            act.wait_ge(gath, n)
            a.activation(xs_hi[:], ps[:, 5:7, :].rearrange("p a (b c) -> p (a b) c", c=P), ACT.Copy).then_inc(xhi, 1)

        gather_hi(1)
        hi_to(S_MOE)
        act.wait_ge(routed, 1)
        n_items = act.value_load(table[0:1, EXTRA_MAX:EXTRA_MAX + 1], min_val=E, max_val=E + EXTRA_MAX)

        with act.Fori(0, n_items) as i:
            def e_up(j, s=None):
                k = i * N_FFN if s is None else i * N_FFN + s * 6
                turn = i * (N_FFN // RAW) if s is None else i * (N_FFN // RAW) + s
                hi_loop(U_MOE, S_MOE, j, turn, k)

            def e_silu_step(s):
                act.wait_ge(split_used, i * N_FFN + (S_MOE + 2) if s is None else i * N_FFN + s * 6 + (S_MOE - 2 + 2))
                act.wait_ge(e_mu, i * NSTEP + 1 if s is None else i * NSTEP + s + 1)
                a.activation(e_silu[:], ps[:, 0, :], ACT.Silu).then_inc(e_si, 1)

            def gt_split(n):
                act.wait_ge(e_tr, n)
                a.activation(gt_hi[:], ps[:, 2, :].rearrange("p (a b) -> p a b", b=P), ACT.Copy).then_inc(e_hi, 1)

            e_up(0)
            e_up(1)
            act.wait_ge(split_used, i * N_FFN + S_MOE)
            act.wait_ge(scat_add, i * KD + 1)
            a.activation(e_y[:], ps[:, 3:5, :].rearrange("p a c -> p (a c)"), ACT.Copy).then_inc(y_cp, 1)
            e_up(2)
            e_up(3)
            e_silu_step(None)
            with act.Fori(1, NSTEP) as s:
                for j in range(4):
                    e_up(j - 2, s)
                gt_split(i * NSTEP + s)
                for j in range(4, 6):
                    e_up(j - 2, s)
                e_silu_step(s)
            gather_hi(i + 2)
            gt_split(i * NSTEP + NSTEP)
            act.wait_ge(gat_tr, i + 1)
            a.activation(gatT[:], ps[:, 1, 0:T], ACT.Copy).then_inc(gat_cp, 1)
            for j in range(2):
                e_up(4 + 6 * 6 + j)
        act.wait_ge(split_used, n_items * N_FFN + S_MOE)
        a.activation(e_y[:], ps[:, 3:5, :].rearrange("p a c -> p (a c)"), ACT.Copy).then_inc(y_end, 1)

        for k in range(0, KD, 2):
            act.wait_ge(x_new, 12 + k // 2 + 1)
            a.activation(sq[:, k:k + 2, :], x[:, k:k + 2, :], ACT.Square).then_inc(sq_ready, 1)
        std(8, 0, D)
        act.wait_ge(v_stored, 32 * DEPTH)
        for b in range(NBLK):
            n = BLK[b]
            act.wait_ge(fin_tr, b + 1)
            a.activation(xtok[0:n, b, :], ps[0:n, 2 + 2 * b:4 + 2 * b, :].rearrange("p a c -> p (a c)"),
                         ACT.Copy).then_inc(fin_cp, 1)

    @block.vector
    def _(ve):
        v = nc.vector
        steps = [0]
        cur = [0]

        def step(ins):
            steps[0] += 1
            ins.then_inc(dve, 1)
            ve.wait_ge(dve, steps[0])

        def lo(s):
            u = U_OF_SPLIT[s]
            ve.wait_ge(hi_ready, s + 1)
            v.tensor_tensor(w_lo[:, s % SPL], raw[:, u % RAW], w_hi[:, s % SPL].bitcast(F32),
                            ALU.subtract).then_inc(lo_ready, 1)

        def lo_loop(u0, s0, j, per):
            ve.wait_ge(hi_ready, per + (s0 + j + 1))
            v.tensor_tensor(w_lo[:, (s0 + j) % SPL], raw[:, (u0 + j) % RAW], w_hi[:, (s0 + j) % SPL].bitcast(F32),
                            ALU.subtract).then_inc(lo_ready, 1)

        def lo_to(s):
            while cur[0] < s:
                lo(cur[0])
                cur[0] += 1

        ve.wait_ge(prep_tr, 1)
        v.tensor_copy(cT[:], ps[:, 0, 0:KD * ROWS].rearrange("p (k r) -> p k r", r=ROWS)).then_inc(prep_cp, 1)
        ve.wait_ge(prep_tr, 2)
        v.tensor_copy(vec[:], ps[:, 1, 0:DEPTH * NV].rearrange("p (l n) -> p l n", n=NV)).then_inc(prep_cp, 1)
        for k in range(KD):
            ve.wait_ge(prep_tr, 3 + k)
            v.tensor_copy(x[:, k, :], ps[:, 2 + k % 2, 0:T]).then_inc(x_cp, 1)
        for l in range(DEPTH):
            ve.wait_ge(prep_tr, 11 + l)
            v.tensor_copy(gw[:, l], ps[:, 4, :].rearrange("p (h t) -> p h t", t=P))
            v.tensor_copy(gs[:, l], ps[:, 5, 0:H * NS_TOK].rearrange("p (h t) -> p h t", t=NS_TOK)
                          ).then_inc(prep_cp, 1)
        for l in range(DEPTH):
            ve.wait_ge(prep_tr, 13 + l)
            v.tensor_copy(sp_[:, l, :, :, 0:BUF],
                          ps[:, 4, 0:H * NSEQ * BUF].rearrange("p (g b r) -> p g b r", g=H, r=BUF)).then_inc(prep_cp, 1)
        ve.wait_ge(const, 1)
        ve.wait_ge(zeroed, 1)
        for gi, w in enumerate(WIN):
            ins = v.tensor_scalar(first[:, gi, :], iota[:, 0:PADP], 1.0, float(w), ALU.add, ALU.min)
        step(ins)
        step(v.reciprocal(rcnt[:], first[:]))

        def ada_add(l, c):
            ve.wait_ge(row_tr, BLOCK[l, c] + 1)
            v.tensor_tensor(mod[:, l, 4 * c:4 * c + 4, :],
                            ps[:, 5, 0:4 * ROWS].rearrange("p (m r) -> p m r", r=ROWS),
                            vec[:, l, R_ADAB + 4 * c:R_ADAB + 4 * c + 4].unsqueeze(2).to_broadcast([P, 4, ROWS]),
                            ALU.add).then_inc(mod_add, 1)

        def ada_gain(l, which):
            ve.wait_ge(mod_add, BLOCK[l, 6 * which + 3] + 1)
            r = (R_N1, R_N2)[which]
            c = (3 * which + 1) * KD
            step(v.scalar_tensor_tensor(out=gain[:, l, which], in0=mod[:, l, c:c + KD, :], scalar=1.0,
                                        in1=vec[:, l, r:r + KD].unsqueeze(2).to_broadcast([P, KD, ROWS]),
                                        op0=ALU.add, op1=ALU.mult))

        def norm(l, which):
            n = 2 * l + which
            ve.wait_ge(std_ready, 4 * l + 3 * which + 1)
            step(v.reciprocal(rstd[:], stdt[:]))

            def scale_pair(b):
                k = 2 * b
                step(v.tensor_tensor(hf[:, k:k + 2, :], x[:, k:k + 2, :],
                                     rstd[:].unsqueeze(1).to_broadcast([P, 2, T]), ALU.mult))
                smp_v = hf[:, k:k + 2, NP_TOK:T].rearrange("p k (b t) -> p k b t", t=TS)
                gn = gain[:, l, which, k:k + 2, 1:ROWS].unsqueeze(3).to_broadcast([P, 2, NSEQ, TS])
                sh = mod[:, l, 3 * KD * which + k:3 * KD * which + k + 2, 1:ROWS].unsqueeze(3).to_broadcast(
                    [P, 2, NSEQ, TS])
                step(v.tensor_tensor(smp_v, smp_v, gn, ALU.mult))
                v.tensor_tensor(smp_v, smp_v, sh, ALU.add).then_inc(scaled, 1)

            for b in range(KD // 2 + 1):
                if b < KD // 2:
                    scale_pair(b)
                if b >= 1 and n < 3:
                    k = 2 * b - 2
                    ve.wait_ge(hhi, 4 * n + b)
                    ve.wait_ge(scaled, 4 * n + b)
                    v.tensor_tensor(h_lo[:, k:k + 2, 0:T], hf[:, k:k + 2, :], h_hi[:, k:k + 2, 0:T].bitcast(F32),
                                    ALU.subtract).then_inc(h_ready, 1)

        def project_in(l):
            s = S_IN[l]
            lo_to(s + 5)
            ve.wait_ge(v_out, l + 1)
            if l:
                ve.wait_ge(v_stored, 32 * l)
            for j in range(NBLK * H):
                ins = v.bn_stats(v_stat[:, j, :], v_gelu[:, j // H, (j % H) * P:(j % H + 1) * P])
            step(ins)
            for j in range(NBLK * H):
                ins = v.bn_aggr(v_mv[:, j, :], v_stat[:, j, :])
            ins.then_inc(v_var, 1)
            lo_to(s + 6)
            ve.wait_ge(v_sd, l + 1)
            ve.wait_ge(layer_in, 64 * (l + 1))
            ve.wait_ge(v_var, l + 1)
            step(v.reciprocal(v_rstd[:], v_std[:]))
            for j in range(NBLK * H):
                cols = slice((j % H) * P, (j % H + 1) * P)
                ins = v.tensor_scalar(v_norm[:, j // H, cols], v_gelu[:, j // H, cols], v_mv[:, j, 0:1],
                                      v_rstd[:, j:j + 1], ALU.subtract, ALU.mult)
            step(ins)
            step(v.tensor_tensor(v_norm[:], v_norm[:], vng[:].unsqueeze(1).to_broadcast([P, NBLK, HALF]),
                                 ALU.mult))
            v.tensor_tensor(v_norm[:], v_norm[:], vnb[:].unsqueeze(1).to_broadcast([P, NBLK, HALF]),
                            ALU.add).then_inc(v_done, 1)

        def pooled(l):
            ve.wait_ge(p_out, 2 * (l + 1))
            n, src = PADP + NP_TOK, pp
            for j, w in enumerate(WIN):
                dst, half, lo_ = (wb if j % 2 else wa), w // 2, PADP - (16 - w)
                step(v.tensor_tensor(dst[:, j:, lo_:n], src[:, j:, lo_:n], src[:, j:, lo_ - half:n - half], ALU.add))
                src = dst
            ve.wait_ge(win_s, l + 1)
            for j, w in enumerate(WIN):
                ws, wss = (wa, wsa) if j % 2 == 0 else (wb, wsb)
                dj, djs = (wb, wsb) if j % 2 == 0 else (wa, wsa)
                v.scalar_tensor_tensor(out=dj[:, j, 2 * PADP:], in0=ws[:, j, 2 * PADP:], scalar=1.0 / w,
                                       in1=pp[:, j, 2 * PADP:], op0=ALU.mult, op1=ALU.subtract)
                v.scalar_tensor_tensor(out=djs[:, j, :, BUF:], in0=wss[:, j, :, BUF:], scalar=1.0 / w,
                                       in1=sp_[:, l, j, :, BUF:], op0=ALU.mult, op1=ALU.subtract)
                ins = v.tensor_tensor(first[:, j, :], ws[:, j, PADP:2 * PADP], rcnt[:, j, :], ALU.mult)
            step(ins)
            for j in range(H):
                dj = wb if j % 2 == 0 else wa
                ins = v.tensor_tensor(dj[:, j, PADP:2 * PADP], first[:, j, :], pp[:, j, PADP:2 * PADP], ALU.subtract)
            ins.then_inc(d_done, 1)

        def branch(l, n_std, src, k0, row, n_mix):
            ve.wait_ge(std_ready, n_std)
            step(v.reciprocal(rstd[:], stdt[:]))
            for k in range(H):
                ins = v.scalar_tensor_tensor(out=hf[:, k0 + k, :], in0=src[:, k, :],
                                             scalar=vec[:, l, row + k:row + k + 1], in1=rstd[:],
                                             op0=ALU.mult, op1=ALU.mult)
                if k % 2:
                    ins.then_inc(mixed, 1)
            for k in range(0, H, 2):
                ve.wait_ge(mixed_hi, n_mix + k // 2 + 1)
                v.tensor_tensor(h_lo[:, k0 + k:k0 + k + 2, 0:T], hf[:, k0 + k:k0 + k + 2, :],
                                h_hi[:, k0 + k:k0 + k + 2, 0:T].bitcast(F32), ALU.subtract).then_inc(h_ready, 1)

        def mixer(l):
            f = MIXER_MOD[l]
            ve.wait_ge(gate_mm, l + 1)
            v.tensor_tensor(uT[:], uT[:], ps[:, 0:H, 0:T], ALU.mult).then_inc(ya_done, 1)
            pooled(l)
            branch(l, 4 * l + 2, uT, 0, R_AG, 4 * l)
            ada_add(*f[0])
            ada_add(*f[1])
            branch(l, 4 * l + 3, yb, H, R_BG, 4 * l + 2)
            for key in f[2:]:
                ada_add(*key)
            ada_gain(l, 1)

        pairs = [0]

        def residual(l, mod_chunk, k, src):
            gt = mod[:, l, mod_chunk + k:mod_chunk + k + 2, :]
            for q in range(2):
                v.scalar_tensor_tensor(out=x[:, k + q, 0:NP_TOK], in0=src[:, q, 0:NP_TOK], scalar=gt[:, q, 0:1],
                                       in1=x[:, k + q, 0:NP_TOK], op0=ALU.mult, op1=ALU.add)
            if pairs[0]:
                ve.wait_ge(x_new, pairs[0])
            step(v.tensor_tensor(smp[:].rearrange("p k (b t) -> p k b t", t=TS),
                                 src[:, :, NP_TOK:T].rearrange("p k (b t) -> p k b t", t=TS),
                                 gt[:, :, 1:ROWS].unsqueeze(3).to_broadcast([P, 2, NSEQ, TS]), ALU.mult))
            v.tensor_tensor(x[:, k:k + 2, NP_TOK:T], x[:, k:k + 2, NP_TOK:T], smp[:], ALU.add).then_inc(x_new, 1)
            pairs[0] += 1

        def project_out(l):
            s = S_OUT[l]
            lo_to(s + 4)
            for c in range(2):
                ve.wait_ge(split_used, s + 2 * c + 2)
                for m in (0, 2):
                    residual(l, 2 * KD, 4 * c + m, ps[:, 4 * c + m:4 * c + m + 2, :])

        for key in FIRST_MOD:
            ada_add(*key)
        ada_gain(0, 0)
        norm(0, 0)
        project_in(0)
        mixer(0)
        project_out(0)
        norm(0, 1)
        for key in NORM_MOD[1]:
            ada_add(*key)
        ada_gain(1, 0)

        def ffn_mul(used, n):
            ve.wait_ge(split_used, used)
            ve.wait_ge(f_silu, n)
            v.tensor_tensor(g_f[:], silu_t[:], ps[:, KB:2 * KB, 0:T], ALU.mult).then_inc(f_mul, 1)

        def ffn_lo(n):
            ve.wait_ge(f_hi, n)
            ve.wait_ge(f_mul, n)
            v.tensor_tensor(g_lo[:], g_f[:], g_hi[:].bitcast(F32), ALU.subtract).then_inc(f_lo, 1)

        def ffn_add(c, used, own):
            ve.wait_ge(split_used, used)
            ve.wait_ge(f_add, own)
            half = facc[:, 4 * c:4 * c + 4, :]
            v.tensor_tensor(half, half, ps[:, 4 * c:4 * c + 4, 0:T], ALU.add).then_inc(f_add, 1)

        s0, s1, u1 = S_FFN, S_FFN + 4, U_FFN + 4
        v.memset(facc[:], 0.0).then_inc(f_add, 1)
        lo_to(s0 + 4)
        ffn_mul(s0 + 4, 1)
        lo_to(s0 + 6)
        ffn_lo(1)
        with ve.Fori(1, NSTEP - 1) as s:
            per = (s - 1) * 6
            for j in range(2, 6):
                lo_loop(u1, s1, j, per)
            ffn_mul(per + (s1 + 4), s + 1)
            ffn_add(0, per + (s1 + 5), s * 2 - 1)
            lo_loop(u1, s1, 6, per)
            lo_loop(u1, s1, 7, per)
            ffn_add(1, per + (s1 + 6), s * 2)
            ffn_lo(s + 1)
        cur[0] = s1 + 6 * 5 + 2
        lo_to(cur[0] + 4)
        ffn_mul(s1 + 34, 7)
        ffn_add(0, s1 + 35, 11)
        ffn_add(1, s1 + 36, 12)
        lo_to(cur[0] + 2)
        ffn_lo(7)
        ffn_add(0, s1 + 37, 13)
        ffn_add(1, s1 + 38, 14)
        ve.wait_ge(f_add, 15)
        for k in range(0, KD, 2):
            residual(0, 5 * KD, k, facc[:, k:k + 2, :])

        norm(1, 0)
        for key in NORM_MOD[2]:
            ada_add(*key)
        project_in(1)
        mixer(1)
        project_out(1)
        norm(1, 1)

        for b in range(NBLK):
            n = BLK[b]
            ve.wait_ge(log_mm, 1)
            ins = v.tensor_copy(logit[0:n, b, :], ps[0:n, 0, b * E:(b + 1) * E])
        step(ins)
        for b in range(NBLK):
            ins = v.max(top[:, b, :], logit[:, b, :])
        step(ins)
        for b in range(NBLK):
            ins = v.max_index(topi[:, b, :], top[:, b, :], logit[:, b, :])
        step(v.tensor_tensor(dtop[:], top[:, :, 1], top[:, :, 0], ALU.subtract))
        v.nop().then_inc(top_done, 1)
        step(v.tensor_copy(topf[:], topi[:]))
        for j in range(2):
            ins = v.tensor_tensor(oh[:, j], iota[:, 0:E].unsqueeze(1).to_broadcast([P, NBLK, E]),
                                  topf[:, :, j].unsqueeze(2).to_broadcast([P, NBLK, E]), ALU.is_equal)
        step(ins)
        v.tensor_tensor(chosen[:], oh[:, 0], oh[:, 1], ALU.add).then_inc(chosen_r, 1)
        for b in range(NBLK):
            n = BLK[b]
            ve.wait_ge(tok_hi, b + 1)
            v.tensor_tensor(ht_lo[0:n, b, :], ps[0:n, 2 + 2 * b:4 + 2 * b, :].rearrange("p a c -> p (a c)"),
                            ht_hi[0:n, b, :].bitcast(F32), ALU.subtract).then_inc(tok_lo, 1)
        ve.wait_ge(exp_done, 1)
        step(v.tensor_scalar(dsum[:], etop[:], 1.0, None, ALU.add))
        step(v.reciprocal(gate[:, 0], dsum[:]))
        v.tensor_tensor(gate[:, 1], etop[:], gate[:, 0], ALU.mult)
        ve.wait_ge(rank_mm, 1)
        v.memset(rank[:], 0.0)
        step(v.tensor_copy(cnt[:], ps[:, 1, NBLK * E:NBLK * E + E]))
        for b in range(NBLK):
            n = BLK[b]
            ins = v.tensor_copy(rank[0:n, b, :], ps[0:n, 1, b * E:(b + 1) * E])
        step(ins)
        v.tensor_scalar(ext[:], cnt[:], float(P), None, ALU.is_gt)
        step(v.tensor_scalar(ext2[:], cnt[:], float(2 * P), None, ALU.is_gt))
        step(v.tensor_tensor(ext[:], ext[:], ext2[:], ALU.add))
        step(v.memset(ebase[:], 0.0))
        for e in range(1, E):
            step(v.tensor_tensor(ebase[:, e:e + 1], ebase[:, e - 1:e], ext[:, e - 1:e], ALU.add))
        step(v.tensor_tensor(eoff[:], ebase[:], iota[:, 0:E], ALU.subtract))
        step(v.tensor_scalar(eoff[:], eoff[:], float(E - 1), float(P), ALU.add, ALU.mult))
        v.tensor_scalar(over1[:], rank[:], float(P), None, ALU.is_ge)
        step(v.tensor_scalar(posn[:], iota[:, 0:E].unsqueeze(1).to_broadcast([P, NBLK, E]), float(P), None,
                             ALU.mult))
        step(v.tensor_tensor(posn[:], posn[:], rank[:], ALU.add))
        step(v.tensor_tensor(over1[:], over1[:], eoff[:].unsqueeze(1).to_broadcast([P, NBLK, E]), ALU.mult))
        step(v.tensor_tensor(posn[:], posn[:], over1[:], ALU.add))
        for j in range(2):
            step(v.tensor_tensor(tmpe[:], oh[:, j], posn[:], ALU.mult))
            step(v.tensor_reduce(pos[:, j], tmpe[:], AX.X, ALU.add))
        step(v.memset(tab[:], 0.0))
        step(v.tensor_tensor(ext2[:], ebase[:], ext[:], ALU.add))
        for j in range(EXTRA_MAX):
            v.tensor_scalar(inj[:], ebase[:], float(j), None, ALU.is_le)
            step(v.tensor_scalar(inj2[:], ext2[:], float(j), None, ALU.is_gt))
            step(v.tensor_tensor(inj[:], inj[:], inj2[:], ALU.mult))
            step(v.tensor_tensor(inj[:], inj[:], iota[:, 0:E], ALU.mult))
            step(v.tensor_reduce(tab[:, j:j + 1], inj[:], AX.X, ALU.add))
        step(v.tensor_scalar(tab[:, EXTRA_MAX:], ext2[:, E - 1:E], float(E), None, ALU.add))
        v.tensor_copy(table[:], tab[:]).then_inc(routed, 1)

        def select_tokens():
            for b in range(NBLK):
                ins = v.tensor_scalar(gat1[:, b, :], iota[:], pos[:, 0, b:b + 1], None, ALU.is_equal)
            return ins

        def select_second():
            for b in range(NBLK):
                ins = v.scalar_tensor_tensor(out=sel[:, b, :], in0=iota[:], scalar=pos[:, 1, b:b + 1],
                                             in1=gat1[:, b, :], op0=ALU.is_equal, op1=ALU.add)
            return ins

        step(select_tokens())
        select_second().then_inc(sel_ready, 1)

        def gather_lo(n):
            ve.wait_ge(gath, n)
            for q, bank in ((0, 7), (1, 0)):
                ins = v.tensor_copy(xs_lo[:, 4 * q:4 * q + 4, :], ps[:, bank, :].rearrange("p (b c) -> p b c", c=P))
            ins.then_inc(xlo, 1)

        gather_lo(1)
        v.memset(ps[:, 3:5, :], 0.0)
        v.memset(gatT[:], 0.0)
        v.memset(facc[:], 0.0).then_inc(scat_add, 1)
        v.memset(e_g[:], 0.0).then_inc(e_mu, 1)
        lo_to(S_MOE)
        ve.wait_ge(routed, 1)
        n_items = ve.value_load(table[0:1, EXTRA_MAX:EXTRA_MAX + 1], min_val=E, max_val=E + EXTRA_MAX)

        with ve.Fori(0, n_items) as i:
            def e_lo_unit(j, s=None):
                lo_loop(U_MOE, S_MOE, j, i * N_FFN if s is None else i * N_FFN + s * 6)

            def e_mul(s):
                if s is None:
                    ve.wait_ge(split_used, i * N_FFN + (S_MOE + 4))
                    ve.wait_ge(e_si, i * NSTEP + 1)
                else:
                    ve.wait_ge(split_used, i * N_FFN + s * 6 + (S_MOE - 2 + 4))
                    ve.wait_ge(e_si, i * NSTEP + s + 1)
                v.tensor_tensor(e_g[:], e_silu[:], ps[:, 1, :], ALU.mult).then_inc(e_mu, 1)

            def gt_split(n):
                ve.wait_ge(e_hi, n)
                v.tensor_tensor(gt_lo[:], ps[:, 2, :].rearrange("p (a b) -> p a b", b=P),
                                gt_hi[:].bitcast(F32), ALU.subtract).then_inc(e_lo, 1)

            for j in range(4):
                e_lo_unit(j)
            for k in range(KD):
                ve.wait_ge(scat, i * KD + k + 1)
                v.tensor_tensor(facc[:, k, :], facc[:, k, :], ps[:, 5 + k % 3, 0:T], ALU.add).then_inc(scat_add, 1)
            e_mul(None)
            G = 3
            for b in range(NBLK):
                v.tensor_scalar(gat1[:, b, :], iota[:], pos[:, 0, b:b + 1], gate[:, 0, b:b + 1],
                                ALU.is_equal, ALU.mult)
                ins = v.tensor_scalar(gat[:, b, :], iota[:], pos[:, 1, b:b + 1], gate[:, 1, b:b + 1],
                                      ALU.is_equal, ALU.mult)
            ins.then_inc(own, 1)
            ve.wait_ge(own, i * G + 1)
            v.tensor_tensor(gat[:], gat[:], gat1[:], ALU.add).then_inc(gat_step, 1)
            v.tensor_scalar(pos[:], pos[:], -float(P), None, ALU.add).then_inc(own, 1)
            ve.wait_ge(own, i * G + 2)
            ve.wait_ge(gat_step, i + 1)
            select_tokens().then_inc(own, 1)
            ve.wait_ge(own, i * G + 3)
            select_second().then_inc(sel_ready, 1)
            with ve.Fori(1, NSTEP) as s:
                for j in range(4):
                    e_lo_unit(j - 2, s)
                gt_split(i * NSTEP + s)
                for j in range(4, 6):
                    e_lo_unit(j - 2, s)
                e_mul(s)
            gather_lo(i + 2)
            gt_split(i * NSTEP + NSTEP)
            for j in range(2):
                e_lo_unit(4 + 6 * 6 + j)
        for k in range(KD):
            ve.wait_ge(scat_end, k + 1)
            ins = v.tensor_tensor(facc[:, k, :], facc[:, k, :], ps[:, 5 + k % 3, 0:T], ALU.add)
            ins.then_inc(add_end, 1)
        ve.wait_ge(add_end, KD)
        for k in range(0, KD, 2):
            residual(1, 5 * KD, k, facc[:, k:k + 2, :])

        ve.wait_ge(std_ready, 9)
        step(v.reciprocal(rstd[:], stdt[:]))
        for k in range(KD):
            v.scalar_tensor_tensor(out=hf[:, k, :], in0=x[:, k, :], scalar=vec[:, 0, R_FG + k:R_FG + k + 1],
                                   in1=rstd[:], op0=ALU.mult, op1=ALU.mult).then_inc(fin_t, 1)

    @block.tensor
    def _(pe):
        t_ = nc.tensor

        def mm3(out, a_hi, a_lo, b_hi, b_lo, first_, last_):
            t_.matmul(out, a_hi, b_hi, start=first_, stop=False)
            t_.matmul(out, a_hi, b_lo, start=False, stop=False)
            return t_.matmul(out, a_lo, b_hi, start=False, stop=last_)

        pe.wait_ge(const, 1)
        pe.wait_ge(act_c, 1)
        for k in range(KD):
            ins = t_.transpose(ps[:, 0, k * ROWS:(k + 1) * ROWS], cs_row[:, k * P:(k + 1) * P], ident[0:ROWS, 0:ROWS])
        ins.then_inc(prep_tr, 1)
        pe.wait_ge(vec_in, 16 * N_VEC)
        for l in range(DEPTH):
            ins = t_.transpose(ps[:, 1, l * NV:(l + 1) * NV], vrow[:, l, :], ident[0:NV, 0:NV])
        ins.then_inc(prep_tr, 1)
        pe.wait_ge(x_in, 16 * N_X)
        for k in range(KD):
            if k >= 2:
                pe.wait_ge(x_cp, k - 1)
            for b in range(NBLK):
                n = BLK[b]
                ins = t_.transpose(ps[:, 2 + k % 2, b * P:b * P + n], xtok[0:n, b, k * P:(k + 1) * P],
                                   ident[0:n, 0:n])
            ins.then_inc(prep_tr, 1)

        def ada(l, c):
            n = BLOCK[l, c]
            if n >= 2:
                pe.wait_ge(row_out, n - 1)
            for r in range(2):
                u = U_OF_PLAIN[2 * n + r]
                pe.wait_ge(raw_in[u % RAW], 16 * (u // RAW + 1))
                for k in range(KB):
                    ins = t_.matmul(ps[0:ROWS, 6 + n % 2, :], cT[:, r * KB + k, :], raw[:, u % RAW, k, :],
                                    start=(r == 0 and k == 0), stop=(r == 1 and k == KB - 1))
                ins.then_inc(plain_used, 1)

        def ada_tr(l, c):
            n = BLOCK[l, c]
            pe.wait_ge(row_out, n + 1)
            if n >= 1:
                pe.wait_ge(mod_add, n)
            for m in range(4):
                ins = t_.transpose(ps[:, 5, m * ROWS:(m + 1) * ROWS],
                                   modrow[:, m * P:(m + 1) * P], ident[0:ROWS, 0:ROWS])
            ins.then_inc(row_tr, 1)

        def ada_run(blocks, before=None):
            for key in blocks:
                ada(*key)
                if before:
                    ada_tr(*before)
                before = key
            return before

        pe.wait_ge(prep_cp, 1)
        ada(0, 0)
        ada(0, 1)
        pe.wait_ge(aux_in, 16 * (2 * NSEQ + 1))
        pe.wait_ge(gw_in, 16)
        for l in range(DEPTH):
            if l:
                pe.wait_ge(prep_cp, 3)
            for h in range(H):
                t_.transpose(ps[:, 4, h * P:(h + 1) * P], gw_raw[:, l * H + h, :], ident[:])
                ins = t_.transpose(ps[:, 5, h * NS_TOK:(h + 1) * NS_TOK], gs_raw[0:NS_TOK, l * H + h, :],
                                   ident[0:NS_TOK, 0:NS_TOK])
            ins.then_inc(prep_tr, 1)

        def buffers(l, bank):
            for gi in range(H):
                n = NSEQ * BUF
                ins = t_.transpose(ps[:, bank, gi * n:(gi + 1) * n], buf_raw[0:NSEQ * BUF, l, gi * P:(gi + 1) * P],
                                   ident[0:n, 0:n])
            ins.then_inc(prep_tr, 1)

        pe.wait_ge(prep_cp, 4)
        buffers(0, 4)
        pe.wait_ge(prep_cp, 5)
        buffers(1, 4)
        pe.wait_ge(prep_cp, 6)
        ada_tr(0, 0)
        ada_tr(*ada_run([(0, 2), (0, 3)], (0, 1)))

        def sum_squares(n_sq, k0, k1, bank):
            for k in range(k0, k1):
                if k % 2 == 0:
                    pe.wait_ge(sq_ready, n_sq + (k - k0) // 2 + 1)
                ins = t_.matmul(ps[:, bank, 0:T], ones[:], sq[:, k, :], start=(k == k0), stop=(k == k1 - 1))
            ins.then_inc(ssum, 1)

        def unit(s):
            pe.wait_ge(lo_ready, s + 1)
            return w_hi[:, s % SPL], w_lo[:, s % SPL]

        def project_in(l):
            s = S_IN[l]
            for c in range(3):
                if c == 2:
                    pe.wait_ge(u_out, l + 1)
                for r in range(2):
                    wh, wl = unit(s + 2 * c + r)
                    for k in range(KB):
                        kk = r * KB + k
                        if c == 0:
                            pe.wait_ge(h_ready, 12 * l + kk // 2 + 1)
                        if c == 1:
                            for b in range(NBLK):
                                tk = slice(VBLK[b], VBLK[b] + P)
                                ins = mm3(ps[:, 4 + b, :], h_hi[:, kk, tk], h_lo[:, kk, tk], wh[:, k, :], wl[:, k, :],
                                          kk == 0, kk == KD - 1)
                        else:
                            for m in range(4):
                                mc = slice(m * P, (m + 1) * P)
                                out = ps[:, m, 0:T]
                                t_.matmul(out, wh[:, k, mc], h_hi[:, kk, 0:T], start=(kk == 0), stop=False)
                                t_.matmul(out, wh[:, k, mc], h_lo[:, kk, 0:T], start=False, stop=False)
                                ins = t_.matmul(out, wl[:, k, mc], h_hi[:, kk, 0:T], start=False, stop=(kk == KD - 1))
                    ins.then_inc(split_used, 1)

        def state_rows(l):
            pe.wait_ge(p_out, 2 * (l + 1))
            pe.wait_ge(v_out, l + 1)
            for gi in range(H):
                ins = t_.transpose(ps[0:NEWROWS, 4, gi * P:(gi + 1) * P], sps[:, gi, :], ident[:])
            ins.then_inc(st_tr, 1)

        def mix_gate(l):
            pe.wait_ge(masked, 1)
            pe.wait_ge(v_done, l + 1)
            pe.wait_ge(layer_in, 64 * (l + 1))
            for h in range(H):
                hc = slice(h * P, (h + 1) * P)
                bias_one = ones[BIAS_ROW:BIAS_ROW + 1, :]
                for n in range(2):
                    tk = slice(n * P, (n + 1) * P)
                    t_.matmul(ps[:, h, tk], v_norm[:, n, hc], gw[:, l, h, :], start=True, stop=False)
                    t_.matmul(ps[:, h, tk], bias_one, g_bias[:, h, :], start=False, stop=True)
                tk = slice(NP_TOK, T)
                t_.matmul(ps[:, h, tk], v_norm[NS_TOK:P, 2, hc], gs[NS_TOK:P, l, h, :], start=True, stop=False)
                ins = t_.matmul(ps[:, h, tk], bias_one,
                                g_bias[:, h, 0:TS].unsqueeze(1).to_broadcast([1, NSEQ, TS]),
                                start=False, stop=True)
            ins.then_inc(gate_mm, 1)

        def mix_pool(l):
            pe.wait_ge(d_done, l + 1)
            pe.wait_ge(st_cp, l + 1)
            for gi in range(H):
                if gi:
                    pe.wait_ge(yb_done, H * l + gi)
                dj, djs = (wb, wsb) if gi % 2 == 0 else (wa, wsa)
                t_.matmul(ps[:, 4, 0:NP_TOK], pw[:, gi, :], dj[:, gi, PADP:], start=True, stop=True)
                t_.matmul(ps[:, 4, NP_TOK:T], pw[:, gi, :], djs[:, gi, :, BUF:], start=True,
                          stop=True).then_inc(pool_mm, 1)

        def mixer(l):
            f = MIXER_MOD[l]
            state_rows(l)
            mix_gate(l)
            ada(*f[0])
            pe.wait_ge(ya_done, l + 1)
            sum_squares(12 * l + 4, 0, H, 0)
            last = ada_run(f[1:3], f[0])
            mix_pool(l)
            last = ada_run(f[3:4], last)
            sum_squares(12 * l + 6, H, KD, 4)
            ada_tr(*ada_run(f[4:], last))

        def project_out(l):
            s = S_OUT[l]
            for c in range(2):
                for r in range(2):
                    wh, wl = unit(s + 2 * c + r)
                    pe.wait_ge(h_ready, 12 * l + 4 + 2 * (r + 1))
                    for k in range(KB):
                        kk = r * KB + k
                        for m in range(4):
                            mc = slice(m * P, (m + 1) * P)
                            out = ps[:, 4 * c + m, 0:T]
                            t_.matmul(out, wh[:, k, mc], h_hi[:, kk, 0:T], start=(kk == 0), stop=False)
                            t_.matmul(out, wh[:, k, mc], h_lo[:, kk, 0:T], start=False, stop=False)
                            ins = t_.matmul(out, wl[:, k, mc], h_hi[:, kk, 0:T], start=False, stop=(kk == KD - 1))
                    ins.then_inc(split_used, 1)

        sum_squares(0, 0, KD, 0)
        project_in(0)
        mixer(0)
        pe.wait_ge(mod_add, BLOCK[MIXER_MOD[0][-1]] + 1)
        project_out(0)
        sum_squares(8, 0, KD, 0)
        ada_tr(*ada_run(NORM_MOD[1]))
        pe.wait_ge(mod_add, BLOCK[NORM_MOD[1][-1]] + 1)

        def up(base, u, s, wh, wl, r, bank0):
            for k in range(KB):
                kk = r * KB + k
                for m in range(4):
                    mc = slice(m * P, (m + 1) * P)
                    out = ps[:, bank0 + m, 0:T]
                    t_.matmul(out, wh[:, k, mc], h_hi[:, kk, 0:T], start=(kk == 0), stop=False)
                    t_.matmul(out, wh[:, k, mc], h_lo[:, kk, 0:T], start=False, stop=False)
                    ins = t_.matmul(out, wl[:, k, mc], h_hi[:, kk, 0:T], start=False, stop=(kk == KD - 1))
            ins.then_inc(split_used, 1)

        def down(wh, wl, bank0):
            for k in range(KB):
                for m in range(4):
                    mc = slice(m * P, (m + 1) * P)
                    out = ps[:, bank0 + m, 0:T]
                    t_.matmul(out, wh[:, k, mc], g_hi[:, k, :], start=(k == 0), stop=False)
                    t_.matmul(out, wh[:, k, mc], g_lo[:, k, :], start=False, stop=False)
                    ins = t_.matmul(out, wl[:, k, mc], g_hi[:, k, :], start=False, stop=(k == KB - 1))
            ins.then_inc(split_used, 1)

        def ffn_unit(j, per):
            pe.wait_ge(lo_ready, per + (S_FFN + 4 + j + 1))
            sl = (S_FFN + 4 + j) % SPL
            return w_hi[:, sl], w_lo[:, sl]

        pe.wait_ge(h_ready, 12)
        for j in range(4):
            up(None, None, None, *unit(S_FFN + j), j % 2, 4 * (j // 2))

        def ffn_down(s):
            pe.wait_ge(f_lo, s)

        with pe.Fori(1, NSTEP) as s:
            per = (s - 1) * 6
            for j in range(4):
                if j == 0:
                    pe.wait_ge(f_add, s * 2 - 1)
                    pe.wait_ge(f_silu, s)
                if j == 2:
                    pe.wait_ge(f_add, s * 2 - 1)
                    pe.wait_ge(f_mul, s)
                    pe.wait_ge(f_add, s * 2 - 1)
                up(None, None, None, *ffn_unit(j, per), j % 2, 4 * (j // 2))
            ffn_down(s)
            pe.wait_ge(f_silu, s + 1)
            down(*ffn_unit(4, per), 0)
            pe.wait_ge(f_mul, s + 1)
            down(*ffn_unit(5, per), 4)
        pe.wait_ge(f_add, 13)
        pe.wait_ge(f_lo, 7)
        down(*unit(S_FFN + 40), 0)
        down(*unit(S_FFN + 41), 4)

        sum_squares(12, 0, KD, 0)
        ada_tr(*ada_run(NORM_MOD[2]))
        pe.wait_ge(mod_add, BLOCK[NORM_MOD[2][-1]] + 1)
        project_in(1)
        mixer(1)
        pe.wait_ge(mod_add, BLOCK[MIXER_MOD[1][-1]] + 1)
        project_out(1)
        sum_squares(20, 0, KD, 0)

        pe.wait_ge(rw_in, 16)
        pe.wait_ge(scaled, 16)
        pe.wait_ge(affine, 32)
        for b in range(NBLK):
            n = BLK[b]
            for k in range(KD):
                ins = t_.matmul(ps[0:n, 0, b * E:(b + 1) * E], hf[:, k, b * P:b * P + n], rw[:, k, :],
                                start=(k == 0), stop=(k == KD - 1))
        ins.then_inc(log_mm, 1)
        for b in range(NBLK):
            n = BLK[b]
            for k in range(KD):
                ins = t_.transpose(ps[0:n, 2 + 2 * b + k // 4, (k % 4) * P:(k % 4 + 1) * P],
                                   hf[:, k, b * P:b * P + n], ident[:])
            ins.then_inc(tok_tr, 1)
        pe.wait_ge(chosen_r, 1)
        for b in range(NBLK):
            n = BLK[b]
            for q in range(b):
                t_.matmul(ps[0:n, 1, b * E:(b + 1) * E], ones[:, 0:n], chosen[:, q, :], start=(q == 0), stop=False)
            t_.matmul(ps[0:n, 1, b * E:(b + 1) * E], below[0:n, 0:n], chosen[0:n, b, :], start=(b == 0), stop=True)
        for b in range(NBLK):
            n = BLK[b]
            ins = t_.matmul(ps[:, 1, NBLK * E:(NBLK + 1) * E], ones[0:n, :], chosen[0:n, b, :], start=(b == 0),
                            stop=(b == NBLK - 1))
        ins.then_inc(rank_mm, 1)

        def gather():
            for src, banks in ((ht_hi, (5, 6)), (ht_lo, (7, 0))):
                for k in range(KD):
                    out = ps[:, banks[k // 4], (k % 4) * P:(k % 4 + 1) * P]
                    for b in range(NBLK):
                        n = BLK[b]
                        ins = t_.matmul(out, src[0:n, b, k * P:(k + 1) * P], sel[0:n, b, :], start=(b == 0),
                                        stop=(b == NBLK - 1))
            ins.then_inc(gath, 1)

        pe.wait_ge(tok_lo, NBLK)
        pe.wait_ge(sel_ready, 1)
        gather()
        pe.wait_ge(routed, 1)
        n_items = pe.value_load(table[0:1, EXTRA_MAX:EXTRA_MAX + 1], min_val=E, max_val=E + EXTRA_MAX)

        with pe.Fori(0, n_items) as i:
            def e_unit(j, s=None):
                k = i * N_FFN if s is None else i * N_FFN + s * 6
                pe.wait_ge(lo_ready, k + (S_MOE + j + 1))
                return w_hi[:, (S_MOE + j) % SPL], w_lo[:, (S_MOE + j) % SPL]

            def e_up(w, r, bank):
                for k in range(KB):
                    kk = r * KB + k
                    ins = mm3(ps[:, bank, :], xs_hi[:, kk, :], xs_lo[:, kk, :], w[0][:, k, :], w[1][:, k, :],
                              kk == 0, kk == KD - 1)
                ins.then_inc(split_used, 1)

            def e_transpose(n):
                pe.wait_ge(e_mu, n + 1)
                for m in range(KB):
                    ins = t_.transpose(ps[:, 2, m * P:(m + 1) * P], e_g[:, m * P:(m + 1) * P], ident[:])
                ins.then_inc(e_tr, 1)

            def e_down(w, c, first_, last_):
                for k in range(KB):
                    ins = mm3(ps[:, 3 + c, :], gt_hi[:, k, :], gt_lo[:, k, :], w[0][:, k, :], w[1][:, k, :],
                              first_ and k == 0, last_ and k == KB - 1)
                ins.then_inc(split_used, 1)

            def e_step(s, j0, sreg, first_):
                pe.wait_ge(e_si, i * NSTEP + s)
                e_up(e_unit(j0, sreg), 0, 0)
                e_up(e_unit(j0 + 1, sreg), 1, 0)
                e_transpose(i * NSTEP + s)
                e_up(e_unit(j0 + 2, sreg), 0, 1)
                e_up(e_unit(j0 + 3, sreg), 1, 1)
                pe.wait_ge(e_lo, i * NSTEP + s)
                for c in range(2):
                    e_down(e_unit(j0 + 4 + c, sreg), c, first_, False)

            pe.wait_ge(xhi, i + 1)
            pe.wait_ge(xlo, i + 1)
            for j in range(4):
                if j == 2:
                    pe.wait_ge(y_cp, i + 1)
                    pe.wait_ge(scat_add, i * KD + 1)
                    for k in range(KD):
                        if k >= 3:
                            pe.wait_ge(scat_add, i * KD + k - 1)
                        t_.matmul(ps[:, 5 + k % 3, 0:T], e_y[:, k * P:(k + 1) * P], gatT[:], start=True,
                                  stop=True).then_inc(scat, 1)
                e_up(e_unit(j), j % 2, j // 2)
            e_step(1, 4, None, True)
            with pe.Fori(2, NSTEP) as s:
                e_step(s, -2, s, False)
            pe.wait_ge(sel_ready, i + 2)
            pe.wait_ge(e_si, i * NSTEP + NSTEP)
            gather()
            e_transpose(i * NSTEP + NSTEP)
            pe.wait_ge(gat_step, i + 1)
            for b in range(NBLK):
                n = BLK[b]
                ins = t_.transpose(ps[:, 1, b * P:b * P + n], gat[0:n, b, :], ident[0:n, 0:n])
            ins.then_inc(gat_tr, 1)
            pe.wait_ge(e_lo, i * NSTEP + NSTEP)
            for c in range(2):
                e_down(e_unit(40 + c), c, False, True)
            pe.wait_ge(gat_cp, i + 1)
            pe.wait_ge(xhi, i + 2)
            pe.wait_ge(xlo, i + 2)
        pe.wait_ge(y_end, 1)
        for k in range(KD):
            if k >= 3:
                pe.wait_ge(add_end, k - 2)
            t_.matmul(ps[:, 5 + k % 3, 0:T], e_y[:, k * P:(k + 1) * P], gatT[:], start=True,
                      stop=True).then_inc(scat_end, 1)

        sum_squares(24, 0, KD, 0)
        pe.wait_ge(fin_t, KD)
        for b in range(NBLK):
            n = BLK[b]
            for k in range(KD):
                ins = t_.transpose(ps[0:n, 2 + 2 * b + k // 4, (k % 4) * P:(k % 4 + 1) * P],
                                   hf[:, k, b * P:b * P + n], ident[:])
            ins.then_inc(fin_tr, 1)


def kernel(**inputs):
    import concourse.bacc as bacc
    from concourse.bass_utils import run_bass_kernel_spmd
    nc = bacc.Bacc("TRN2", target_bir_lowering=False, num_devices=1, dynamic_dma_scratch_size=1024)
    build_program(nc)
    arrays = {f"in_{n}": np.ascontiguousarray(a) for n, a in inputs.items()}
    r = run_bass_kernel_spmd(nc, [arrays], core_ids=[0]).results[0]
    return tuple(r[f"out_{i}"] for i in range(6))
```
